# Optimizing a Trainium2 kernel written in Bass

```python
import math
import jax, jax.numpy as jnp
from jax import lax
import numpy as np

D_MODEL = 1024
BATCH = 1
SEQ = 128
DEPTH = 2
DEC_BATCH = 1
DEC_SEQ = 128
PAST_LEN = 128

GRID_W = 64
N_EVEN = (DEPTH + 1) // 2
N_ODD = DEPTH // 2
N_HEADS_A = D_MODEL // 256
HEAD_DIM_A = 64
VAL_DIM_A = 2 * HEAD_DIM_A
MIX_A = N_HEADS_A * VAL_DIM_A
QK_W = N_HEADS_A * 2 * HEAD_DIM_A
SG_GROUPS = 4
SG_CHUNK = 128
SG_DIM = (D_MODEL - MIX_A) // SG_GROUPS
MIX_B = SG_GROUPS * SG_DIM
IN_W = 2 * QK_W + MIX_A + 2 * MIX_B
POOL_WINDOWS = (2, 4, 8, 16)
POOL_DIM = D_MODEL // len(POOL_WINDOWS)
N_EXPERTS = 16
N_EXPERT_GROUPS = 4
EXPERTS_PER_GROUP = N_EXPERTS // N_EXPERT_GROUPS
TOP_K = 2
D_FF_EXPERT = D_MODEL // 2
ROPE_BASE = 10000.0
Q_BLOCK = 128
N_MOD = 6
EPS = 1e-6

kernel_name = 'hybrid_diffusion_prefix_trunk_step'

def rms_norm(x, g):
    xf = x.astype(jnp.float32)
    y = xf * lax.rsqrt(jnp.mean(xf * xf, axis=-1, keepdims=True) + EPS)
    return (y * g.astype(jnp.float32)).astype(x.dtype)

def lambda_init(layer_idx):
    return 0.8 - 0.6 * math.exp(-0.3 * layer_idx)

def rope_2d(x):
    S = x.shape[1]
    rows = S // GRID_W
    row = jnp.repeat(jnp.arange(rows), GRID_W)
    col = jnp.tile(jnp.arange(GRID_W), rows)
    half = HEAD_DIM_A // 2
    nf = half // 2
    inv = ROPE_BASE ** (-jnp.arange(nf, dtype=jnp.float32) / nf)

    def rot(xa, pos):
        ang = pos.astype(jnp.float32)[:, None] * inv[None, :]
        cos = jnp.cos(ang)[:, None, None, :]
        sin = jnp.sin(ang)[:, None, None, :]
        x1, x2 = xa[..., :nf], xa[..., nf:]
        return jnp.concatenate([x1 * cos - x2 * sin, x2 * cos + x1 * sin], axis=-1)

    xf = x.astype(jnp.float32)
    out = jnp.concatenate([rot(xf[..., :half], row), rot(xf[..., half:], col)], axis=-1)
    return out.astype(x.dtype)

def diff_attention(q, k, v, lam):
    B, Sq = q.shape[0], q.shape[1]
    nq = Sq // Q_BLOCK
    qb = jnp.moveaxis(q.reshape(B, nq, Q_BLOCK, N_HEADS_A, 2, HEAD_DIM_A), 1, 0)
    scale = HEAD_DIM_A ** -0.5

    def block(qi):
        s = jnp.einsum('bqhcd,bkhcd->bhcqk', qi, k, preferred_element_type=jnp.float32) * scale
        p = jax.nn.softmax(s, axis=-1)
        a = (p[:, :, 0] - lam * p[:, :, 1]).astype(v.dtype)
        return jnp.einsum('bhqk,bkhe->bqhe', a, v)

    o = lax.map(block, qb)
    return jnp.moveaxis(o, 0, 1).reshape(B, Sq, N_HEADS_A, VAL_DIM_A)

def spatial_gate(u, v, sg_w, sg_b):
    B, S, _ = u.shape
    nc = S // SG_CHUNK
    u = jax.nn.gelu(u).reshape(B, nc, SG_CHUNK, SG_GROUPS, SG_DIM)
    v = jax.nn.gelu(v).reshape(B, nc, SG_CHUNK, SG_GROUPS, SG_DIM)
    mixed = jnp.einsum('gpq,bnqgc->bnpgc', sg_w, v) + sg_b.T[None, None, :, :, None]
    return (u * mixed).reshape(B, S, MIX_B)

def pool_mixer(h, pool_w, pool_scale):
    B, S, D = h.shape
    hf = h.astype(jnp.float32)
    cs = jnp.concatenate([jnp.zeros((B, 1, D), jnp.float32), jnp.cumsum(hf, axis=1)], axis=1)
    t = jnp.arange(S)
    outs = []
    for g, w in enumerate(POOL_WINDOWS):
        lo = jnp.clip(t - w // 2, 0, S)
        hi = jnp.clip(t - w // 2 + w, 0, S)
        csg = cs[:, :, g * POOL_DIM:(g + 1) * POOL_DIM]
        mean = (csg[:, hi] - csg[:, lo]) / (hi - lo).astype(jnp.float32)[None, :, None]
        d = (mean - hf[:, :, g * POOL_DIM:(g + 1) * POOL_DIM]).astype(h.dtype)
        outs.append(d @ pool_w[g])
    return jnp.concatenate(outs, axis=-1) * pool_scale

def moe(h, router_w, router_b, w_gate, w_up, w_down):
    B, S, D = h.shape
    t = h.reshape(B * S, D)
    scores = jax.nn.sigmoid(jnp.einsum('td,de->te', t, router_w, preferred_element_type=jnp.float32))
    sel = scores + router_b.astype(jnp.float32)
    grp_score = lax.top_k(sel.reshape(-1, N_EXPERT_GROUPS, EXPERTS_PER_GROUP), TOP_K)[0].sum(-1)
    g_idx = jnp.argmax(grp_score, axis=-1)
    in_grp = (jnp.arange(N_EXPERTS) // EXPERTS_PER_GROUP)[None, :] == g_idx[:, None]
    _, e_idx = lax.top_k(jnp.where(in_grp, sel, -jnp.inf), TOP_K)
    wts = jnp.take_along_axis(scores, e_idx, axis=-1)
    wts = wts / jnp.sum(wts, axis=-1, keepdims=True)
    gates = jnp.sum(jax.nn.one_hot(e_idx, N_EXPERTS, dtype=jnp.float32) * wts[..., None], axis=1)
    g = jnp.einsum('td,edf->tef', t, w_gate)
    u = jnp.einsum('td,edf->tef', t, w_up)
    a = jax.nn.silu(g) * u * gates[:, :, None].astype(t.dtype)
    return jnp.einsum('tef,efd->td', a, w_down).reshape(B, S, D)

def trunk(x, cond, ctx_k, ctx_v, norm1_g, norm2_g, w_ada, b_ada, w_in, w_out, q_norm_g, k_norm_g,
          lam_q1, lam_k1, lam_q2, lam_k2, subln_g, sg_w, sg_b, pool_w, pool_scale,
          router_w, router_b, w_gate, w_up, w_down):
    latent = ctx_k is not None
    B, S, _ = x.shape
    ks, vs = [], []
    for l in range(DEPTH):
        mod = jax.nn.silu(cond) @ w_ada[l] + b_ada[l]
        sh1, sc1, g1, sh2, sc2, g2 = [m[:, None, :] for m in jnp.split(mod, N_MOD, axis=-1)]
        h = rms_norm(x, norm1_g[l]) * (1 + sc1) + sh1
        if l % 2 == 0:
            e = l // 2
            proj = h @ w_in[e]
            q = proj[..., :QK_W].reshape(B, S, N_HEADS_A, 2, HEAD_DIM_A)
            k = proj[..., QK_W:2 * QK_W].reshape(B, S, N_HEADS_A, 2, HEAD_DIM_A)
            v = proj[..., 2 * QK_W:2 * QK_W + MIX_A].reshape(B, S, N_HEADS_A, VAL_DIM_A)
            gu = proj[..., 2 * QK_W + MIX_A:2 * QK_W + MIX_A + MIX_B]
            gv = proj[..., 2 * QK_W + MIX_A + MIX_B:]
            q = rms_norm(q, q_norm_g[e])
            k = rms_norm(k, k_norm_g[e])
            if latent:
                qa = rope_2d(q)
                keys = jnp.concatenate([ctx_k[:, e], rope_2d(k)], axis=1)
                vals = jnp.concatenate([ctx_v[:, e], v], axis=1)
            else:
                qa, keys, vals = q, k, v
                ks.append(k)
                vs.append(v)
            lam0 = lambda_init(l)
            lam = (jnp.exp(jnp.sum(lam_q1[e].astype(jnp.float32) * lam_k1[e].astype(jnp.float32)))
                   - jnp.exp(jnp.sum(lam_q2[e].astype(jnp.float32) * lam_k2[e].astype(jnp.float32))) + lam0)
            att = rms_norm(diff_attention(qa, keys, vals, lam), subln_g[e]) * (1.0 - lam0)
            sgo = spatial_gate(gu, gv, sg_w[e], sg_b[e])
            out = jnp.concatenate([att.reshape(B, S, MIX_A), sgo], axis=-1) @ w_out[e]
        else:
            o = l // 2
            out = pool_mixer(h, pool_w[o], pool_scale[o])
        x = x + g1 * out
        h = rms_norm(x, norm2_g[l]) * (1 + sc2) + sh2
        x = x + g2 * moe(h, router_w, router_b, w_gate[l], w_up[l], w_down[l])
    return x, ks, vs

def setup_inputs(seed: int = 0) -> dict:
    key = jax.random.key(seed)
    k = jax.random.split(key, 32)
    f32 = jnp.float32

    def nrm(kk, shape, s):
        return jax.random.normal(kk, shape, f32) * s

    D = D_MODEL
    return {
        'x_prompt': nrm(k[0], (BATCH, SEQ, D), 1.0),
        'x_sample': nrm(k[1], (DEC_BATCH, DEC_SEQ, D), 1.0),
        'cache_k': nrm(k[2], (DEC_BATCH, N_EVEN, PAST_LEN, N_HEADS_A, 2, HEAD_DIM_A), 1.0),
        'cache_v': nrm(k[3], (DEC_BATCH, N_EVEN, PAST_LEN, N_HEADS_A, VAL_DIM_A), 1.0),
        'c': nrm(k[4], (DEC_BATCH, D), 1.0),
        'c_ctx': nrm(k[5], (D,), 1.0),
        'norm1_g': 1.0 + nrm(k[6], (DEPTH, D), 0.02),
        'norm2_g': 1.0 + nrm(k[7], (DEPTH, D), 0.02),
        'w_ada': nrm(k[8], (DEPTH, D, N_MOD * D), 0.5 * D ** -0.5),
        'b_ada': nrm(k[9], (DEPTH, N_MOD * D), 0.01),
        'w_in': nrm(k[10], (N_EVEN, D, IN_W), D ** -0.5),
        'w_out': nrm(k[11], (N_EVEN, MIX_A + MIX_B, D), (MIX_A + MIX_B) ** -0.5),
        'q_norm_g': 1.0 + nrm(k[12], (N_EVEN, HEAD_DIM_A), 0.02),
        'k_norm_g': 1.0 + nrm(k[13], (N_EVEN, HEAD_DIM_A), 0.02),
        'lam_q1': nrm(k[14], (N_EVEN, HEAD_DIM_A), 0.1),
        'lam_k1': nrm(k[15], (N_EVEN, HEAD_DIM_A), 0.1),
        'lam_q2': nrm(k[16], (N_EVEN, HEAD_DIM_A), 0.1),
        'lam_k2': nrm(k[17], (N_EVEN, HEAD_DIM_A), 0.1),
        'subln_g': 1.0 + nrm(k[18], (N_EVEN, VAL_DIM_A), 0.02),
        'sg_w': nrm(k[19], (N_EVEN, SG_GROUPS, SG_CHUNK, SG_CHUNK), 0.5 * SG_CHUNK ** -0.5),
        'sg_b': 1.0 + nrm(k[20], (N_EVEN, SG_GROUPS, SG_CHUNK), 0.02),
        'pool_w': nrm(k[21], (N_ODD, len(POOL_WINDOWS), POOL_DIM, POOL_DIM), POOL_DIM ** -0.5),
        'pool_scale': 1.0 + nrm(k[22], (N_ODD, D), 0.02),
        'router_w': nrm(k[23], (D, N_EXPERTS), D ** -0.5),
        'router_b': nrm(k[24], (N_EXPERTS,), 0.01),
        'w_gate': nrm(k[25], (DEPTH, N_EXPERTS, D, D_FF_EXPERT), D ** -0.5),
        'w_up': nrm(k[26], (DEPTH, N_EXPERTS, D, D_FF_EXPERT), D ** -0.5),
        'w_down': nrm(k[27], (DEPTH, N_EXPERTS, D_FF_EXPERT, D), D_FF_EXPERT ** -0.5),
    }

def reference(x_prompt, x_sample, cache_k, cache_v, c, c_ctx, norm1_g, norm2_g, w_ada, b_ada,
              w_in, w_out, q_norm_g, k_norm_g, lam_q1, lam_k1, lam_q2, lam_k2, subln_g,
              sg_w, sg_b, pool_w, pool_scale, router_w, router_b, w_gate, w_up, w_down):
    y_prompt, ks, vs = trunk(x_prompt, c_ctx[None, :], None, None, norm1_g, norm2_g, w_ada, b_ada,
                             w_in, w_out, q_norm_g, k_norm_g, lam_q1, lam_k1, lam_q2, lam_k2,
                             subln_g, sg_w, sg_b, pool_w, pool_scale, router_w, router_b,
                             w_gate, w_up, w_down)
    state_k = jnp.stack(ks, axis=1)
    state_v = jnp.stack(vs, axis=1)
    y_sample, _, _ = trunk(x_sample, c, cache_k, cache_v, norm1_g, norm2_g, w_ada, b_ada,
                           w_in, w_out, q_norm_g, k_norm_g, lam_q1, lam_k1, lam_q2, lam_k2,
                           subln_g, sg_w, sg_b, pool_w, pool_scale, router_w, router_b,
                           w_gate, w_up, w_down)
    return (y_prompt, y_sample, state_k, state_v)


_drawn_inputs = setup_inputs


def setup_inputs(seed=0):
    import zlib

    import numpy as np

    out = dict(_drawn_inputs(seed))
    spreads = {}
    factors = {'norm1_g': 2.794,
     'q_norm_g': 6.941,
     'k_norm_g': 2.824,
     'lam_q1': 8.088,
     'subln_g': 18.556,
     'pool_scale': 18.377,
     'cache_k': 8.0,
     'cache_v': 8.0,
     'norm2_g': 2.834,
     'sg_b': 4.816}
    for name, (base, spread) in spreads.items():
        noise = np.random.default_rng([zlib.crc32(name.encode()), seed]).standard_normal(out[name].shape)
        drawn = base * np.exp(spread * noise) if base else spread * noise
        out[name] = __import__('jax').numpy.asarray(drawn.astype(out[name].dtype))
    for name, factor in factors.items():
        out[name] = (out[name] * factor).astype(out[name].dtype)
    return out
```

```python
from contextlib import ExitStack
import math

import numpy as np
import concourse.bass as bass
from concourse import mybir

F32 = mybir.dt.float32
I32 = mybir.dt.int32
ALU = mybir.AluOpType
ACT = mybir.ActivationFunctionType
AX_X = mybir.AxisListType.X

P = 128
D = 1024
KD = D // P
NS = 2
H, DH = 4, 64
NE = 16
FF = 512
KF = FF // P
CAP = 64
NTILE = NS * P // CAP
SLOT = 4096
NSLOT = 9
LAM0 = 0.8 - 0.6 * math.exp(0.0)
EPS = 1e-6
BIG = 1.0e30
GRID_W = 64
WINDOWS = (2, 4, 8, 16)
SH1, SC1, G1, SH2, SC2, G2 = range(6)

C_ID, C_UP, C_ONE, C_POOL = 0, 128, 256, 384
C_SEL = C_POOL + 4 * P
C_CMP = C_SEL + 2 * P
C_IOTA = C_CMP + 32
C_RANK = C_IOTA + NTILE * CAP
C_COS = C_RANK + 20
C_SIN = C_COS + 64
C_N = C_SIN + 64


def constant_table():
    t = np.zeros((P, C_N), np.float32)
    i = np.arange(P)
    t[:, C_ID:C_ID + P] = np.eye(P)
    t[:, C_UP:C_UP + P] = i[:, None] < i[None, :]
    t[:, C_ONE:C_ONE + P] = 1.0
    for g, w in enumerate(WINDOWS):
        lo = np.clip(i - w // 2, 0, P)
        hi = np.clip(i - w // 2 + w, 0, P)
        band = ((i[:, None] >= lo[None, :]) & (i[:, None] < hi[None, :])) / (hi - lo)[None, :].astype(np.float32)
        t[:, C_POOL + g * P:C_POOL + (g + 1) * P] = band - np.eye(P)
    for s in range(NS):
        t[:, C_SEL + s * P:C_SEL + (s + 1) * P] = (i % 32 == s)[:, None]
        t[:, C_CMP + s] = i % 32 == s
    t[:, C_IOTA:C_IOTA + NTILE * CAP] = np.arange(NTILE * CAP)
    t[:, C_RANK:C_RANK + 16] = 16 - np.arange(16)
    t[:, C_RANK + 16:C_RANK + 20] = 4 - np.arange(4)
    inv = np.float32(10000.0) ** (-np.arange(16, dtype=np.float32) / 16)
    for half, pos in enumerate((i // GRID_W, i % GRID_W)):
        ang = pos.astype(np.float32)[:, None] * inv[None, :]
        for part, sign in ((0, -1.0), (1, 1.0)):
            c = half * 32 + part * 16
            t[:, C_COS + c:C_COS + c + 16] = np.cos(ang)
            t[:, C_SIN + c:C_SIN + c + 16] = sign * np.sin(ang)
    return t


def ring_plan():
    filled, last = [0] * NSLOT, [None] * NSLOT
    units, before = {}, []
    first = [("ada", u) for u in range(4)] + [("win", u) for u in range(5)] \
        + [("ada", u) for u in range(4, 12)] + [("wout", u) for u in range(2)]
    second = [("ada", u) for u in range(12, 24)] + [("pool", 0)]
    for l, (names, at, n) in enumerate(((first, 0, 6), (second, 3, NSLOT))):
        for i, name in enumerate(names):
            slot = (at + i) % n
            filled[slot] += 4 if name[0] == "pool" else 1
            units[name] = (slot, filled[slot], last[slot])
            last[slot] = name
        before.append((list(filled), list(last)))
        last = [None] * NSLOT
        for e in range(NE):
            for j in range(3):
                filled[3 * (e % 3) + j] += 1
    return first, second, units, before


def trunk_kernel(nc, x_prompt, x_sample, cache_k, cache_v, c, c_ctx, norm1_g, norm2_g, w_ada, b_ada,
                 w_in, w_out, q_norm_g, k_norm_g, lam_q1, lam_k1, lam_q2, lam_k2, subln_g,
                 sg_w, sg_b, pool_w, pool_scale, router_w, router_b, w_gate, w_up, w_down, table,
                 y_prompt, y_sample, state_k, state_v):
    first_units, second_units, UNIT, BEFORE = ring_plan()

    with ExitStack() as ctx:
        def sb(name, shape, dt=F32):
            return ctx.enter_context(nc.sbuf_tensor(name, shape, dt))

        def sem(name):
            return ctx.enter_context(nc.semaphore(name))

        ring = sb("ring", [P, NSLOT * SLOT])
        x = sb("x", [P, NS, D])
        h = sb("h", [P, NS, D])
        hT = sb("hT", [P, KD, NS * P])
        modc = sb("modc", [P, 3, 512])
        part = sb("part", [P, 2, 512])
        tab = sb("tab", [P, C_N])
        gam = sb("gam", [P, D])
        bada = sb("bada", [32, 512])
        condT = sb("condT", [P, KD, 32])
        cond = sb("cond", [P, NS, KD])
        rw = sb("rw", [P, KD, NE])
        rb = sb("rb", [P, NE])
        work = sb("work", [P, 2944])
        st = sb("st", [P, 9 * 8])
        rt = sb("rt", [P, 11 * 32 + 48])
        posm = sb("posm", [P, NS, NE + 1])
        gt = sb("gt", [P, NS, NE + 1])
        cnt = sb("cnt", [1, NE], I32)
        vecs = sb("vecs", [P, 6 * 64 + 128 + 4 + 4])
        bank = [ctx.enter_context(nc.psum_tensor(f"bank{i}", [P, 512], F32)) for i in range(8)]

        def col(a, n):
            return tab[:, a:a + n]

        ident, upper, ones = col(C_ID, P), col(C_UP, P), col(C_ONE, P)

        def slot(i, n=SLOT):
            return ring[:, i * SLOT:i * SLOT + n]

        at = [6 * SLOT]

        def take(n):
            at[0] += n
            assert at[0] <= NSLOT * SLOT
            return ring[:, at[0] - n:at[0]]

        qk = take(2048).rearrange("p (s t n) -> p s t n", s=NS, t=2)
        vv = take(1024).rearrange("p (s n) -> p s n", s=NS)
        gu = take(1024).rearrange("p (s n) -> p s n", s=NS)
        gv = take(1024).rearrange("p (s n) -> p s n", s=NS)
        ck = take(512)
        cv = take(512)
        qT = take(1024).rearrange("p (s h t) -> p s h t", s=NS, h=H)
        kTp = take(512).rearrange("p (h t) -> p h t", h=H)
        kTs = take(1024).rearrange("p (h t) -> p h t", h=H)
        prob = [take(1024).rearrange("p (c h t) -> p c h t", c=2, h=H),
                take(2048).rearrange("p (c h t) -> p c h t", c=2, h=H)]
        sgw = work[:, 0:512].rearrange("p (g q) -> p g q", g=4)
        sgwT = work[:, 512:1024].rearrange("p (g q) -> p g q", g=4)
        aTp = work[:, 0:512].rearrange("p (h t) -> p h t", h=H)
        aTs = work[:, 1024:2048].rearrange("p (h r t) -> p h r t", h=H, r=2)
        tmp = work[:, 2048:2560]
        xg = work[:, 0:512].rearrange("p (k s) -> p k s", k=KD)
        act = work[0:CAP, 512:1024]
        actT = work[:, 1024:1280].rearrange("p (k s) -> p k s", k=KF)
        STg = work[:, 1280:1536].rearrange("p (s t) -> p s t", s=NS)
        ysb = work[:, 1536:2048]
        S = work[:, 2560:2688].rearrange("p (s c) -> p s c", s=NS)
        Sg = work[:, 2688:2944].rearrange("p (s c) -> p s c", s=NS)
        pscale = work[:, 0:1024]
        hTf = hT[:, :, :].rearrange("p k t -> p (k t)")
        o_xg = hTf[:, 0:512].rearrange("p (k s) -> p k s", k=KD)
        o_act = hTf[0:CAP, 512:1024]
        o_actT = hTf[:, 1024:1280].rearrange("p (k s) -> p k s", k=KF)
        o_STg = hTf[:, 1280:1536].rearrange("p (s t) -> p s t", s=NS)
        o_S = hTf[:, 1536:1664].rearrange("p (s c) -> p s c", s=NS)
        o_Sg = hTf[:, 1664:1920].rearrange("p (s c) -> p s c", s=NS)
        o_y = gam[:, 0:512]
        qg, kg, lams = vecs[:, 0:64], vecs[:, 64:128], vecs[:, 128:384]
        subg, lamv, sgbT = vecs[:, 384:512], vecs[:, 512:516], vecs[:, 516:520]
        ssq = st[:, 0:8]
        qss = st[:, 8:16]
        oss = st[:, 16:24]
        mx = st[:, 24:40].rearrange("p (s c h) -> p s c h", s=NS, c=2)
        esum = st[:, 40:56].rearrange("p (s c h) -> p s c h", s=NS, c=2)

        w_landed = [sem(f"w_landed{i}") for i in range(NSLOT)]
        first_in, attn_in, gam_in, ps_in = sem("first_in"), sem("attn_in"), sem("gam_in"), sem("ps_in")
        zeroed, cond_ready, lam_dots, lam_exp = sem("zeroed"), sem("cond_ready"), sem("lam_dots"), sem("lam_exp")
        ada_part, pool_done = sem("ada_part"), sem("pool_done")
        ada_evac, ada_comp, mod_ready = sem("ada_evac"), sem("ada_comp"), sem("mod_ready")
        ss_ready, bc_ready, h_ready = sem("ss_ready"), sem("bc_ready"), sem("h_ready")
        gam_used = sem("gam_used")
        tr_psum, tr_done = sem("tr_psum"), sem("tr_done")
        pre_psum, pre_evac = sem("pre_psum"), sem("pre_evac")
        win_psum, win_evac, qk_ready = sem("win_psum"), sem("win_evac"), sem("qk_ready")
        qkT_psum, qkT_dve, qkT_act = sem("qkT_psum"), sem("qkT_dve"), sem("qkT_act")
        sg_psum, sg_used = sem("sg_psum"), sem("sg_used")
        score_psum, mx_ready, exp_ready, a_map = sem("score_psum"), sem("mx_ready"), sem("exp_ready"), sem("a_map")
        aT_psum, aT_sb, o_psum, att_ready = sem("aT_psum"), sem("aT_sb"), sem("o_psum"), sem("att_ready")
        res_ready, res_used, x_ready = sem("res_ready"), sem("res_used"), sem("x_ready")
        logit_psum, router_exp, chosen, pos_psum, routed = (sem("logit_psum"), sem("router_exp"),
                                                            sem("chosen"), sem("pos_psum"), sem("routed"))
        dT_psum, dT_sb = sem("dT_psum"), sem("dT_sb")
        S_ready, Sg_ready, gat_done, xg_ready = sem("S_ready"), sem("Sg_ready"), sem("gat_done"), sem("xg_ready")
        ffn_done, silu_done, act_ready, actT_psum = (sem("ffn_done"), sem("silu_done"), sem("act_ready"),
                                                     sem("actT_psum"))
        actT_ready, ST_psum, ST_ready = sem("actT_ready"), sem("ST_psum"), sem("ST_ready")
        down_done, y_ready, scat_done = sem("down_done"), sem("y_ready"), sem("scat_done")
        ovf_pe, ovf_act, ovf_dve = sem("ovf_pe"), sem("ovf_act"), sem("ovf_dve")
        dve_step = sem("dve_step")
        state_out, y_out = sem("state_out"), sem("y_out")

        block = ctx.enter_context(nc.Block())

        def expert_weights(w, l, e, n):
            flat = w.rearrange("l e (p k) f -> (l e) p (k f)", k=n)
            return flat[bass.ds(NE * l + e, 1), :, :].rearrange("a p n -> p (a n)")

        ada_v = w_ada.rearrange("l (p k) n -> l p k n", k=KD)
        win_v = w_in[0].rearrange("(p k) n -> p k n", k=KD)
        wout_v = w_out[0].rearrange("(p k) n -> p k n", k=KD)
        pool_v = pool_w[0].rearrange("g (j p) n -> p g j n", p=P)

        @block.sync
        def _(eng):
            def wait_used(name):
                kind, u = name
                if kind == "ada":
                    eng.wait_ge(ada_part, u + 1)
                elif kind == "win":
                    eng.wait_ge(win_psum, 2 * u + 2)
                elif kind == "wout":
                    eng.wait_ge(res_ready, u + 3)
                else:
                    eng.wait_ge(pool_done, 1)

            def unit(name):
                i, _, before = UNIT[name]
                kind, u = name
                if before:
                    wait_used(before)
                src = {"ada": lambda: ada_v[u // 12, :, :, 512 * (u % 12):512 * (u % 12) + 512],
                       "win": lambda: win_v[:, :, 512 * u:512 * u + 512],
                       "wout": lambda: wout_v[:, :, 512 * u:512 * u + 512],
                       "pool": lambda: pool_v}[kind]()
                if kind == "pool":
                    for g in range(4):
                        eng.dma_start(slot(i, 2048).rearrange("p (g j n) -> p g j n", g=4, j=2)[:, g],
                                      src[:, g]).then_inc(w_landed[i], 16)
                    return
                eng.dma_start(slot(i).rearrange("p (k n) -> p k n", k=KD), src).then_inc(w_landed[i], 16)

            def load_expert(l, e, buf):
                for j, (w, n) in enumerate(((w_gate, KD), (w_up, KD), (w_down, KF))):
                    eng.dma_start(slot(3 * buf + j), expert_weights(w, l, e, n)).then_inc(w_landed[3 * buf + j], 16)

            for name in first_units:
                unit(name)
            for l in range(2):
                _, last_unit = BEFORE[l]
                for e in range(3):
                    for j in range(3):
                        if last_unit[3 * e + j]:
                            wait_used(last_unit[3 * e + j])
                    if l == 0 and e == 2:
                        eng.wait_ge(att_ready, 2)
                        eng.wait_ge(o_psum, 2)
                        eng.wait_ge(state_out, 32)
                    load_expert(l, e, e)
                eng.wait_ge(down_done, NE * l + 1)
                load_expert(l, 3, 0)
                with eng.Fori(0, 4) as it:
                    for j in range(3):
                        eng.wait_ge(down_done, 3 * it + (NE * l + j + 2))
                        load_expert(l, 3 * it + (4 + j), (j + 1) % 3)
                if l == 0:
                    for n, name in enumerate(second_units):
                        if n < NSLOT:
                            eng.wait_ge(down_done, 14 + n // 3)
                        unit(name)
            for s, y in enumerate((y_prompt, y_sample)):
                eng.wait_ge(x_ready, 7 + s)
                eng.dma_start(y[0], x[:, s, :]).then_inc(y_out, 16)
            eng.wait_ge(y_out, 32)

        @block.gpsimd
        def _(eng):
            eng.wait_ge(qk_ready, 3)
            eng.dma_start(state_k[0, 0].rearrange("t h c d -> t (h c d)"), qk[:, 0, 1, :]).then_inc(state_out, 16)
            eng.wait_ge(win_evac, 5)
            eng.dma_start(state_v[0, 0].rearrange("t h d -> t (h d)"), vv[:, 0, :]).then_inc(state_out, 16)
            eng.wait_ge(state_out, 32)

        def mod_unit(j, hf):
            return 2 * j + hf

        @block.tensor
        def _(eng):
            mm = nc.tensor.matmul

            def ada_partial(a):
                i, fill, _ = UNIT[("ada", a)]
                eng.wait_ge(w_landed[i], 16 * fill)
                if a:
                    eng.wait_ge(ada_evac, a)
                w = slot(i).rearrange("p (k n) -> p k n", k=KD)
                for k in range(KD):
                    g = k % 4
                    last = mm(bank[6][32 * g:32 * g + 32, :], condT[:, k, :], w[:, k, :],
                              start=k < 4, stop=k >= 4, skip_group_check=True)
                last.then_inc(ada_part, 1)

            def ada_compress(a):
                eng.wait_ge(ada_evac, a + 1)
                if a:
                    eng.wait_ge(mod_ready, a)
                g = a % 4
                mm(bank[7][32 * g:32 * g + 32, :], col(C_CMP, 32), part[:, a % 2, :],
                   start=True, stop=False, skip_group_check=True)
                mm(bank[7][32 * g:32 * g + 2, :], ident[0:32, a:a + 1].broadcast_to([32, 2]), bada[:, :],
                   start=False, stop=True, skip_group_check=True).then_inc(ada_comp, 1)

            def ada_blocks(a0, a1):
                for a in range(a0, a1):
                    ada_partial(a)
                    if a > a0:
                        ada_compress(a - 1)
                ada_compress(a1 - 1)

            def broadcast_mod(out, l, j, hf, s):
                u = mod_unit(j, hf)
                g = u % 4
                eng.wait_ge(mod_ready, 12 * l + u + 1)
                return mm(out, tab[32 * g:32 * g + 32, C_SEL + s * P:C_SEL + (s + 1) * P],
                          modc[32 * g:32 * g + 32, u // 4, :], start=True, stop=True)

            def norm_mods(n):
                l, w = n // 2, n % 2
                for cc in range(4):
                    ci, s, hf = 4 * n + cc, cc // 2, cc % 2
                    if cc >= 2:
                        eng.wait_ge(h_ready, ci - 1)
                    b = 2 * (ci % 2)
                    broadcast_mod(bank[b][:, :], l, 3 * w + 1, hf, s)
                    broadcast_mod(bank[b + 1][:, :], l, 3 * w, hf, s).then_inc(bc_ready, 1)

            def transpose_rows(cidx, wait_source):
                for ii in range(4 * cidx, 4 * cidx + 4):
                    s, j = (ii % 4) // 2, ii % 2
                    wait_source(s)
                    if ii >= 2:
                        eng.wait_ge(tr_done, ii - 1)
                    for kk in range(4):
                        last = nc.tensor.transpose(bank[4 + j][:, kk * P:(kk + 1) * P],
                                                   h[:, s, 4 * j + kk::KD], ident)
                    last.then_inc(tr_psum, 1)

            def residual_gates(r, l, j):
                for ri in range(4 * r, 4 * r + 4):
                    if ri % 4 >= 2:
                        eng.wait_ge(res_used, ri - 1)
                    broadcast_mod(bank[4 + ri % 2][:, :], l, j, ri % 2, (ri % 4) // 2).then_inc(res_ready, 1)

            def route(l):
                eng.wait_ge(mod_ready, 12 * (l + 1))
                eng.wait_ge(tr_done, 12 + 4 * l)
                for s in range(NS):
                    for k in range(KD):
                        last = mm(bank[7][:, s * NE:(s + 1) * NE], hT[:, k, s * P:(s + 1) * P], rw[:, k, :],
                                  start=k == 0, stop=k == KD - 1)
                last.then_inc(logit_psum, 1)
                eng.wait_ge(chosen, l + 1)
                m0, m1 = [rt[:, 320 + s * NE:320 + (s + 1) * NE] for s in range(NS)]
                mm(bank[7][:, 64:80], upper, m0, start=True, stop=True)
                mm(bank[7][:, 80:96], ones, m0, start=True, stop=False)
                mm(bank[7][:, 80:96], upper, m1, start=False, stop=True)
                mm(bank[7][:, 96:112], ones, m0, start=True, stop=False)
                mm(bank[7][:, 96:112], ones, m1, start=False, stop=True).then_inc(pos_psum, 1)

            def gather(dst):
                for k in range(KD):
                    for s in range(NS):
                        last = mm(bank[4][:, k * CAP:(k + 1) * CAP], h[:, s, k::KD], dst[:, s, :],
                                  start=s == 0, stop=s == NS - 1)
                return last

            def ffn(buf, xs):
                wg = slot(3 * buf).rearrange("p (k f) -> p k f", k=KD)
                wu = slot(3 * buf + 1).rearrange("p (k f) -> p k f", k=KD)
                for k in range(KD):
                    for q, w in enumerate((wg, wu)):
                        last = mm(bank[5][64 * q:64 * q + CAP, :], xs[:, k, :], w[:, k, :],
                                  start=k == 0, stop=k == KD - 1, skip_group_check=True)
                return last

            def act_transposes(a):
                for k in range(KF):
                    last = nc.tensor.transpose(bank[7][:, 256 + k * CAP:256 + (k + 1) * CAP],
                                               a[:, k::KF], ident[0:CAP, 0:CAP])
                return last

            def scatter_transposes(sg):
                for s in range(NS):
                    last = nc.tensor.transpose(bank[7][:, s * P:(s + 1) * P],
                                               sg[:, s, :], ident)
                return last

            def down(buf, aT):
                wd = slot(3 * buf + 2).rearrange("p (k d) -> p k d", k=KF)
                for k in range(KF):
                    for q in range(2):
                        last = mm(bank[6][64 * q:64 * q + CAP, :], aT[:, k, :], wd[:, k, 512 * q:512 * q + 512],
                                  start=k == 0, stop=k == KF - 1, skip_group_check=True)
                return last

            def scatter(stg, y):
                for s in range(NS):
                    for q in range(2):
                        last = mm(bank[2 * s + q][:, :], stg[64 * q:64 * q + CAP, s, :], y[64 * q:64 * q + CAP, :],
                                  start=False, stop=False, skip_group_check=True)
                return last

            def expert(l, e, buf, landed, first=False):
                n = eng.value_load(cnt[0:1, bass.ds(e, 1)], min_val=0, max_val=NS * P)
                gn, en = 17 * l, NE * l
                for j in range(3):
                    eng.wait_ge(w_landed[3 * buf + j], landed[j])
                eng.wait_ge(xg_ready, e + (gn + 1))
                if not first:
                    eng.wait_ge(act_ready, e + en)
                    eng.wait_ge(actT_ready, e + en)
                    eng.wait_ge(ST_ready, e + en)
                    eng.wait_ge(y_ready, e + en)

                def tile(q):
                    base = 15 * e + (15 * en + 5 * q)
                    eng.wait_ge(ovf_dve, base + 1)
                    gather(o_S).then_inc(ovf_pe, 1)
                    eng.wait_ge(ovf_dve, base + 2)
                    ffn(buf, o_xg).then_inc(ovf_pe, 1)
                    eng.wait_ge(ovf_dve, base + 3)
                    scatter_transposes(o_Sg)
                    act_transposes(o_act).then_inc(ovf_pe, 1)
                    eng.wait_ge(ovf_dve, base + 4)
                    down(buf, o_actT).then_inc(ovf_pe, 1)
                    eng.wait_ge(ovf_dve, base + 5)
                    scatter(o_STg, o_y).then_inc(ovf_pe, 1)

                with eng.If(n > CAP):
                    tile(0)
                    with eng.If(n > 2 * CAP):
                        tile(1)
                        tile(2)
                    with eng.Else():
                        eng.wait_ge(ovf_pe, 15 * e + (15 * en + 5))
                        eng.sem_inc(ovf_pe, 10)
                    eng.nop()
                with eng.Else():
                    eng.sem_inc(ovf_pe, 15)

                ffn(buf, xg).then_inc(ffn_done, 1)
                eng.wait_ge(S_ready, e + (gn + 2))
                gather(S).then_inc(gat_done, 1)
                eng.wait_ge(Sg_ready, e + (en + 1))
                eng.wait_ge(act_ready, e + (en + 1))
                scatter_transposes(Sg).then_inc(ST_psum, 1)
                act_transposes(act).then_inc(actT_psum, 1)
                if not first:
                    scatter(STg, ysb).then_inc(scat_done, 1)
                eng.wait_ge(actT_ready, e + (en + 1))
                down(buf, actT).then_inc(down_done, 1)

            def moe(l):
                filled, _ = BEFORE[l]
                eng.wait_ge(routed, l + 1)
                eng.wait_ge(S_ready, 17 * l + 1)
                eng.wait_ge(h_ready, 4 * (2 * l + 1) + 4)
                for b in range(4):
                    mm(bank[b][:, :], condT[:, 0, 2:3].broadcast_to([P, P]), tab[:, 0:512], start=True, stop=False,
                       skip_group_check=True)
                gather(S).then_inc(gat_done, 1)
                expert(l, 0, 0, [16 * (filled[j] + 1) for j in range(3)], first=True)
                with eng.Fori(0, 5) as it:
                    for j in range(3):
                        buf, nth = (j + 1) % 3, (j + 1) // 3
                        expert(l, 3 * it + (j + 1), buf,
                               [16 * it + 16 * (filled[3 * buf + i] + nth + 1) for i in range(3)])
                eng.wait_ge(y_ready, NE * (l + 1))
                eng.wait_ge(ST_ready, NE * (l + 1))
                scatter(STg, ysb).then_inc(scat_done, 1)

            eng.wait_ge(first_in, 16 * 7)
            eng.wait_ge(cond_ready, 1)
            ada_blocks(0, 4)
            eng.wait_ge(attn_in, 16 * 13)
            for i, src in enumerate((ck.rearrange("p (h t) -> p h t", h=H), sgw)):
                for k in range(4):
                    last = nc.tensor.transpose(bank[2 + i][:, k * P:(k + 1) * P], src[:, k, :], ident)
                last.then_inc(pre_psum, 1)
            eng.wait_ge(pre_evac, 2)
            norm_mods(0)
            transpose_rows(0, lambda s: eng.wait_ge(h_ready, 2 * s + 2))
            for i in range(10):
                u, s = i // 2, i % 2
                sl, fill, _ = UNIT[("win", u)]
                eng.wait_ge(w_landed[sl], 16 * fill)
                eng.wait_ge(tr_done, 2 * s + 2)
                if i >= 2:
                    eng.wait_ge(win_evac, i - 1)
                w = slot(sl).rearrange("p (k n) -> p k n", k=KD)
                for k in range(KD):
                    last = mm(bank[i % 2][:, :], hT[:, k, s * P:(s + 1) * P], w[:, k, :],
                              start=k == 0, stop=k == KD - 1)
                last.then_inc(win_psum, 1)
            eng.wait_ge(win_evac, 10)
            for g in range(4):
                last = mm(bank[g // 2][:, 256 * (g % 2):256 * (g % 2) + 256].rearrange("p (s n) -> p s n", s=NS),
                          sgwT[:, g, :], gv[:, :, g * P:(g + 1) * P], start=True, stop=True)
                if g % 2:
                    last.then_inc(sg_psum, 1)
            for i in range(4):
                s, t = i // 2, i % 2
                eng.wait_ge(qk_ready, (1, 3, 2, 4)[i])
                for hh in range(H):
                    last = nc.tensor.transpose(bank[2 + i][:, hh * P:(hh + 1) * P],
                                               qk[:, s, t, hh * P:(hh + 1) * P], ident)
                last.then_inc(qkT_psum, 1)

            def score(b, s, cmap, heads):
                keys, n = (kTp, P) if s == 0 else (kTs, 2 * P)
                r = slice(64 * cmap, 64 * cmap + 64)
                for q, hh in enumerate(heads):
                    last = mm(bank[b][:, q * n:(q + 1) * n], qT[r, s, hh, :], keys[r, hh, :], start=True, stop=True)
                return last

            eng.wait_ge(sg_used, 4)
            eng.wait_ge(qkT_dve, 2)
            score(0, 0, 0, range(4))
            score(1, 0, 1, range(4)).then_inc(score_psum, 1)
            eng.wait_ge(qkT_act, 2)
            for pair in range(2):
                score(2 + 2 * pair, 1, 0, (2 * pair, 2 * pair + 1))
                score(3 + 2 * pair, 1, 1, (2 * pair, 2 * pair + 1)).then_inc(score_psum, 1)
            ada_blocks(4, 8)
            eng.wait_ge(a_map, 4)
            for hh in range(H):
                last = nc.tensor.transpose(bank[0][:, hh * P:(hh + 1) * P], prob[0][:, 0, hh, :], ident)
            last.then_inc(aT_psum, 1)
            for pair in range(2):
                eng.wait_ge(a_map, 6 + 2 * pair)
                for q in range(4):
                    last = nc.tensor.transpose(bank[1 + pair][:, q * P:(q + 1) * P],
                                               prob[1][:, 0, 2 * pair + q // 2, (q % 2) * P:(q % 2 + 1) * P], ident)
                last.then_inc(aT_psum, 1)
            eng.wait_ge(aT_sb, 1)
            for hh in range(H):
                last = mm(bank[3][:, hh * P:(hh + 1) * P], aTp[:, hh, :], vv[:, 0, hh * P:(hh + 1) * P],
                          start=True, stop=True)
            last.then_inc(o_psum, 1)
            eng.wait_ge(aT_sb, 3)
            for hh in range(H):
                o = bank[4][:, hh * P:(hh + 1) * P]
                mm(o, aTs[:, hh, 0, :], cv[:, hh * P:(hh + 1) * P], start=True, stop=False)
                last = mm(o, aTs[:, hh, 1, :], vv[:, 1, hh * P:(hh + 1) * P], start=False, stop=True)
            last.then_inc(o_psum, 1)
            ada_blocks(8, 12)
            eng.wait_ge(att_ready, 2)
            transpose_rows(1, lambda s: None)
            for ri in range(4):
                s, u = ri // 2, ri % 2
                sl, fill, _ = UNIT[("wout", u)]
                eng.wait_ge(w_landed[sl], 16 * fill)
                eng.wait_ge(tr_done, 6 + 2 * s)
                w = slot(sl).rearrange("p (k n) -> p k n", k=KD)
                for k in range(KD):
                    last = mm(bank[ri][:, :], hT[:, k, s * P:(s + 1) * P], w[:, k, :],
                              start=k == 0, stop=k == KD - 1)
                eng.wait_ge(tr_done, 8)
                if ri >= 2:
                    eng.wait_ge(res_used, ri - 1)
                broadcast_mod(bank[4 + ri % 2][:, :], 0, G1, u, s).then_inc(res_ready, 1)
            eng.wait_ge(res_used, 4)
            norm_mods(1)
            transpose_rows(2, lambda s: eng.wait_ge(h_ready, 4 + 2 * s + 2))
            route(0)
            moe(0)
            residual_gates(1, 0, G2)

            eng.wait_ge(res_used, 8)
            ada_blocks(12, 16)
            norm_mods(2)
            pw = slot(UNIT[("pool", 0)][0], 2048).rearrange("p (g j n) -> p g j n", g=4, j=2)
            for s in range(NS):
                eng.wait_ge(h_ready, 8 + 2 * s + 2)
                for j in range(2):
                    for kk in range(4):
                        ch = 4 * j + kk
                        last = mm(bank[4 + j][:, kk * P:(kk + 1) * P], h[:, s, ch * P:(ch + 1) * P],
                                  col(C_POOL + (ch // 2) * P, P), start=True, stop=True)
                    last.then_inc(dT_psum, 1)
                if s == 0:
                    eng.wait_ge(dT_sb, 2)
            ada_blocks(16, 24)
            sl, fill, _ = UNIT[("pool", 0)]
            eng.wait_ge(w_landed[sl], 16 * fill)
            eng.wait_ge(h_ready, 12)
            for s in range(NS):
                eng.wait_ge(dT_sb, 2 * s + 2)
                for g in range(4):
                    for j in range(2):
                        last = mm(bank[2 * s + g // 2][:, 256 * (g % 2):256 * (g % 2) + 256],
                                  hT[:, 2 * g + j, s * P:(s + 1) * P], pw[:, g, j, :], start=j == 0, stop=j == 1)
            last.then_inc(pool_done, 1)
            eng.wait_ge(dT_sb, 4)
            residual_gates(2, 1, G1)
            eng.wait_ge(res_used, 12)
            norm_mods(3)
            transpose_rows(3, lambda s: eng.wait_ge(h_ready, 12 + 2 * s + 2))
            route(1)
            moe(1)
            residual_gates(3, 1, G2)

        @block.scalar
        def _(eng):
            for dst, src in ((tab[:, :], table[:, :]),
                             (cond[:, 0, :], c_ctx.rearrange("(p k) -> p k", k=KD)),
                             (cond[:, 1, :], c[0].rearrange("(p k) -> p k", k=KD)),
                             (bada[0:24, :], b_ada.rearrange("l (u n) -> (l u) n", n=512)),
                             (bada[24:32, :], b_ada[0].rearrange("(u n) -> u n", n=512)[0:8, :]),
                             (x[:, 0, :], x_prompt[0]), (x[:, 1, :], x_sample[0])):
                eng.dma_start(dst, src).then_inc(first_in, 16)
            eng.dma_start(gam[:, :], norm1_g[0:1, :].broadcast_to([P, D])).then_inc(gam_in, 16)
            for dst, src in ((ck, cache_k[0, 0].rearrange("t h c d -> t (h c d)")),
                             (cv, cache_v[0, 0].rearrange("t h d -> t (h d)")),
                             (sgw, sg_w[0].rearrange("g p q -> p g q")),
                             (qg, q_norm_g[0:1, :].broadcast_to([P, 64])),
                             (kg, k_norm_g[0:1, :].broadcast_to([P, 64])),
                             (lams[:, 0:64], lam_q1[0:1, :].broadcast_to([P, 64])),
                             (lams[:, 64:128], lam_q2[0:1, :].broadcast_to([P, 64])),
                             (lams[:, 128:192], lam_k1[0:1, :].broadcast_to([P, 64])),
                             (lams[:, 192:256], lam_k2[0:1, :].broadcast_to([P, 64])),
                             (subg, subln_g[0:1, :].broadcast_to([P, P])),
                             (sgbT, sg_b[0]),
                             (rb[:, :], router_b.rearrange("(a n) -> a n", a=1).broadcast_to([P, NE])),
                             (rw[:, :, :], router_w.rearrange("(p k) e -> p k e", k=KD))):
                eng.dma_start(dst, src).then_inc(attn_in, 16)

            def evac(dst, b, cols=slice(0, 512)):
                return eng.activation(dst, b[:, cols], ACT.Copy)

            def evac_ada(a):
                eng.wait_ge(ada_part, a + 1)
                if a >= 2:
                    eng.wait_ge(ada_comp, a - 1)
                evac(part[:, a % 2, :], bank[6]).then_inc(ada_evac, 1)

            def evac_mod(a):
                g, u = a % 4, a % 12
                eng.wait_ge(ada_comp, a + 1)
                eng.activation(modc[32 * g:32 * g + 32, u // 4, :], bank[7][32 * g:32 * g + 32, :],
                               ACT.Copy).then_inc(mod_ready, 1)

            def ada_blocks(a0, a1):
                for a in range(a0, a1):
                    evac_ada(a)
                    if a > a0:
                        evac_mod(a - 1)
                evac_mod(a1 - 1)

            def squares(n):
                for s in range(NS):
                    if n:
                        eng.wait_ge(x_ready, 2 * (n - 1) + s + 1)
                    eng.activation(h[:, s, :], x[:, s, :], ACT.Square,
                                   accum_out=ssq[:, 2 * n + s:2 * n + s + 1]).then_inc(ss_ready, 1)

            def evac_transposes(cidx):
                for ii in range(4 * cidx, 4 * cidx + 4):
                    s, j = (ii % 4) // 2, ii % 2
                    eng.wait_ge(tr_psum, ii + 1)
                    eng.activation(hT[:, 4 * j:4 * j + 4, s * P:(s + 1) * P],
                                   bank[4 + j][:, :].rearrange("p (k t) -> p k t", k=4),
                                   ACT.Copy).then_inc(tr_done, 1)

            def expert(l, e, buf, first=False):
                n = eng.value_load(cnt[0:1, bass.ds(e, 1)], min_val=0, max_val=NS * P)
                gn, en = 17 * l, NE * l

                def tile(q):
                    eng.wait_ge(ovf_pe, 15 * e + (15 * en + 5 * q + 2))
                    eng.activation(o_act, bank[5][0:CAP, :], ACT.Silu).then_inc(ovf_act, 1)

                with eng.If(n > CAP):
                    tile(0)
                    with eng.If(n > 2 * CAP):
                        tile(1)
                        tile(2)
                    with eng.Else():
                        eng.wait_ge(ovf_act, 3 * e + (3 * en + 1))
                        eng.sem_inc(ovf_act, 2)
                    eng.nop()
                with eng.Else():
                    eng.sem_inc(ovf_act, 3)

                eng.wait_ge(ffn_done, e + (en + 1))
                if not first:
                    eng.wait_ge(actT_psum, e + en)
                eng.activation(act, bank[5][0:CAP, :], ACT.Silu).then_inc(silu_done, 1)
                eng.wait_ge(gat_done, e + (gn + 2))
                evac(work[:, 0:512], bank[4]).then_inc(xg_ready, 1)
                eng.wait_ge(down_done, e + (en + 1))
                if not first:
                    eng.wait_ge(scat_done, e + en)
                evac(ysb, bank[6]).then_inc(y_ready, 1)

            def moe(l):
                eng.wait_ge(logit_psum, l + 1)
                eng.activation(rt[:, 0:32], bank[7][:, 0:32], ACT.Exp, scale=-1.0).then_inc(router_exp, 1)
                eng.wait_ge(gat_done, 17 * l + 1)
                evac(work[:, 0:512], bank[4]).then_inc(xg_ready, 1)
                eng.wait_ge(routed, l + 1)
                expert(l, 0, 0, first=True)
                with eng.Fori(0, 5) as it:
                    for j in range(3):
                        expert(l, 3 * it + (j + 1), (j + 1) % 3)

            def load_gamma(v, used):
                eng.wait_ge(gam_used, used)
                eng.dma_start(gam[:, :], v.broadcast_to([P, D])).then_inc(gam_in, 16)

            eng.wait_ge(first_in, 16 * 7)
            eng.wait_ge(zeroed, 1)
            eng.activation(condT[:, :, 0:NS].rearrange("p k s -> p s k"), cond[:, :, :],
                           ACT.Silu).then_inc(cond_ready, 1)
            squares(0)
            ada_blocks(0, 4)
            evac_transposes(0)
            for i in range(10):
                u, s = i // 2, i % 2
                eng.wait_ge(win_psum, i + 1)
                dst = (qk[:, s, 0, :], qk[:, s, 1, :], vv[:, s, :], gu[:, s, :], gv[:, s, :])[u]
                eng.activation(dst, bank[i % 2][:, :], ACT.Copy if u < 3 else ACT.Gelu_apprx_tanh).then_inc(win_evac, 1)
            load_gamma(norm2_g[0:1, :], 1)
            for i in (2, 3):
                eng.wait_ge(qkT_psum, i + 1)
                dst = qT[:, 1, :, :] if i == 2 else kTs[:, :, P:2 * P]
                eng.activation(dst, bank[2 + i][:, :].rearrange("p (h t) -> p h t", h=H), ACT.Copy).then_inc(qkT_act, 1)
            eng.wait_ge(lam_dots, 1)
            eng.activation(lamv[:, 2:4], lamv[:, 0:2], ACT.Exp).then_inc(lam_exp, 1)
            for g, (s, b0, heads) in enumerate(((0, 0, range(4)), (1, 2, (0, 1)), (1, 4, (2, 3)))):
                n = P if s == 0 else 2 * P
                eng.wait_ge(mx_ready, g + 1)
                for cm in range(2):
                    for q, hh in enumerate(heads):
                        last = eng.activation(prob[s][:, cm, hh, :], bank[b0 + cm][:, q * n:(q + 1) * n], ACT.Exp,
                                              bias=mx[:, s, cm, hh:hh + 1], scale=DH ** -0.5,
                                              accum_out=esum[:, s, cm, hh:hh + 1])
                last.then_inc(exp_ready, 1)
            ada_blocks(4, 8)
            for i, dst in enumerate((work[:, 0:512], work[:, 1024:1536], work[:, 1536:2048])):
                eng.wait_ge(aT_psum, i + 1)
                evac(dst, bank[i]).then_inc(aT_sb, 1)
            ada_blocks(8, 12)
            evac_transposes(1)
            squares(1)
            evac_transposes(2)
            moe(0)
            eng.wait_ge(scat_done, NE)
            load_gamma(norm1_g[1:2, :], 2)
            eng.wait_ge(y_ready, NE)
            eng.dma_start(pscale, pool_scale[0:1, :].broadcast_to([P, D])).then_inc(ps_in, 16)
            squares(2)
            ada_blocks(12, 16)
            for ii in range(4):
                s, j = ii // 2, ii % 2
                eng.wait_ge(dT_psum, ii + 1)
                eng.activation(hT[:, 4 * j:4 * j + 4, s * P:(s + 1) * P],
                               bank[4 + j][:, :].rearrange("p (k t) -> p k t", k=4), ACT.Copy).then_inc(dT_sb, 1)
            load_gamma(norm2_g[1:2, :], 3)
            ada_blocks(16, 24)
            squares(3)
            evac_transposes(3)
            moe(1)

        @block.vector
        def _(eng):
            steps = [0]

            def chain(ins):
                steps[0] += 1
                ins.then_inc(dve_step, 1)
                eng.wait_ge(dve_step, steps[0])

            def rstd(v, n):
                w = v.shape[1]
                y, t = st[:, 56:56 + w], st[:, 64:64 + w]
                chain(eng.tensor_scalar(v, v, 1.0 / n, EPS, ALU.mult, ALU.add))
                chain(eng.tensor_scalar(t.bitcast(I32), v.bitcast(I32), 1, None, ALU.logical_shift_right))
                chain(eng.tensor_scalar(y.bitcast(I32), t.bitcast(I32), -1.0, float(0x5f3759df), ALU.mult, ALU.add))
                for i in range(3):
                    chain(eng.tensor_tensor(t, y, y, ALU.mult))
                    chain(eng.scalar_tensor_tensor(t, t, -0.5, v, ALU.mult, ALU.mult))
                    chain(eng.scalar_tensor_tensor(v if i == 2 else y, t, 1.5, y, ALU.add, ALU.mult))

            def norm(n):
                eng.wait_ge(gam_in, 16 * (n + 1))
                eng.wait_ge(ss_ready, 2 * n + 2)
                rstd(ssq[:, 2 * n:2 * n + 2], D)
                for s in range(NS):
                    r = ssq[:, 2 * n + s:2 * n + s + 1]
                    for hf in range(2):
                        cs = slice(512 * hf, 512 * hf + 512)
                        hs, b = h[:, s, cs], 2 * (hf % 2)
                        chain(eng.scalar_tensor_tensor(hs, x[:, s, cs], r, gam[:, cs], ALU.mult, ALU.mult))
                        eng.wait_ge(bc_ready, 4 * n + 2 * s + hf + 1)
                        chain(eng.scalar_tensor_tensor(hs, bank[b][:, :], 1.0, hs, ALU.add, ALU.mult))
                        eng.tensor_tensor(hs, hs, bank[b + 1][:, :], ALU.add).then_inc(h_ready, 1)
                        if s == 1 and hf == 1:
                            eng.wait_ge(h_ready, 4 * n + 4)
                            eng.sem_inc(gam_used, 1)

            def residual(r):
                for ri in range(4 * r, 4 * r + 4):
                    s, hf = (ri % 4) // 2, ri % 2
                    cs = slice(512 * hf, 512 * hf + 512)
                    eng.wait_ge(res_ready, ri + 1)
                    ins = eng.tensor_copy(tmp, bank[ri % 4][:, :])
                    chain(ins)
                    ins = eng.tensor_tensor(tmp, tmp, bank[4 + ri % 2][:, :], ALU.mult)
                    ins.then_inc(res_used, 1)
                    eng.wait_ge(res_used, ri + 1)
                    if r == 2:
                        eng.wait_ge(ps_in, 16)
                        chain(eng.tensor_tensor(tmp, tmp, pscale[:, cs], ALU.mult))
                    ins = eng.tensor_tensor(x[:, s, cs], x[:, s, cs], tmp, ALU.add)
                    if hf:
                        ins.then_inc(x_ready, 1)
                        eng.wait_ge(x_ready, 2 * r + s + 1)
                    else:
                        chain(ins)

            def r2(a, n=16):
                return rt[:, a:a + 2 * n].rearrange("p (s e) -> p s e", s=NS)

            def bcast(ap, shape):
                return ap.broadcast_to(shape)

            def first_of(out, v, m, w, rank, n):
                shape = [P, NS, n]
                chain(eng.tensor_reduce(m, v, axis=AX_X, op=ALU.max))
                chain(eng.tensor_tensor(w, v, m.unsqueeze(2).broadcast_to(shape), ALU.is_equal))
                chain(eng.tensor_tensor(w, w, rank.unsqueeze(1).broadcast_to(shape), ALU.mult))
                chain(eng.tensor_reduce(m, w, axis=AX_X, op=ALU.max))
                chain(eng.tensor_tensor(out, w, m.unsqueeze(2).broadcast_to(shape), ALU.is_equal))

            def route(l):
                sc, sel, pair = r2(0), r2(32), rt[:, 64:112].rearrange("p (s g q) -> p s g q", s=NS, g=4)
                gs, w4, g1h = (rt[:, 112 + 8 * i:120 + 8 * i].rearrange("p (s g) -> p s g", s=NS) for i in range(3))
                w16, one1, one2, m = r2(160), r2(192), r2(224), rt[:, 256:258]
                ing, mask = r2(288), r2(320)
                eng.wait_ge(router_exp, l + 1)
                f = rt[:, 0:32]
                chain(eng.tensor_scalar(f, f, 1.0, None, ALU.add))
                chain(eng.reciprocal(f, f))
                chain(eng.tensor_tensor(sel, sc, rb[:, :].unsqueeze(1).broadcast_to([P, NS, NE]), ALU.add))
                v = rt[:, 32:64].rearrange("p (s g e) -> p s g e", s=NS, g=4)
                for s in range(NS):
                    vs, ps = v[:, s], pair[:, s]
                    eng.tensor_tensor(ps[:, :, 0:2], vs[:, :, 0:2], vs[:, :, 2:4], ALU.add)
                    eng.tensor_tensor(ps[:, :, 2:4], vs[:, :, 0:4:2], vs[:, :, 1:4:2], ALU.add)
                    eng.tensor_tensor(ps[:, :, 4:5], vs[:, :, 0:1], vs[:, :, 3:4], ALU.add)
                    chain(eng.tensor_tensor(ps[:, :, 5:6], vs[:, :, 1:2], vs[:, :, 2:3], ALU.add))
                chain(eng.tensor_reduce(gs, pair, axis=AX_X, op=ALU.max))
                first_of(g1h, gs, m, w4, col(C_RANK + 16, 4), 4)
                chain(eng.tensor_copy(ing.rearrange("p s (g e) -> p s g e", g=4),
                                      g1h.unsqueeze(3).broadcast_to([P, NS, 4, 4])))
                chain(eng.tensor_tensor(sel, sel, ing, ALU.mult))
                chain(eng.tensor_scalar(ing, ing, 1.0, BIG, ALU.subtract, ALU.mult))
                chain(eng.tensor_tensor(sel, sel, ing, ALU.add))
                first_of(one1, sel, m, w16, col(C_RANK, 16), 16)
                chain(eng.scalar_tensor_tensor(sel, one1, -4.0 * BIG, sel, ALU.mult, ALU.add))
                first_of(one2, sel, m, w16, col(C_RANK, 16), 16)
                eng.tensor_tensor(mask, one1, one2, ALU.add).then_inc(chosen, 1)
                eng.wait_ge(chosen, l + 1)
                chain(eng.tensor_tensor(w16, mask, sc, ALU.mult))
                chain(eng.tensor_reduce(m, w16, axis=AX_X, op=ALU.add))
                chain(eng.reciprocal(m, m))
                chain(eng.tensor_tensor(gt[:, :, 0:NE], w16, m.unsqueeze(2).broadcast_to([P, NS, NE]), ALU.mult))
                eng.wait_ge(pos_psum, l + 1)
                pp = bank[7][:, 64:96].rearrange("p (s e) -> p s e", s=NS)
                chain(eng.scalar_tensor_tensor(w16, pp, 1.0, mask, ALU.add, ALU.mult))
                chain(eng.tensor_scalar(posm[:, :, 0:NE], w16, 1.0, None, ALU.subtract))
                eng.tensor_copy(cnt[:, :], bank[7][0:1, 96:112]).then_inc(routed, 1)
                eng.wait_ge(routed, l + 1)

            def one_hot(dst, e, q):
                for s in range(NS):
                    last = eng.tensor_scalar(dst[:, s, :], col(C_IOTA + q * CAP, CAP),
                                             posm[:, s, bass.ds(e, 1)], None, ALU.is_equal)
                return last

            def gated_one_hot(dst, e, q):
                for s in range(NS):
                    last = eng.tensor_scalar(dst[:, s, :].rearrange("p (r c) -> p r c", r=2),
                                             col(C_IOTA + q * CAP, CAP).unsqueeze(1).broadcast_to([P, 2, CAP]),
                                             posm[:, s, bass.ds(e, 1)], gt[:, s, bass.ds(e, 1)],
                                             ALU.is_equal, ALU.mult)
                return last

            def expert(l, e, buf, first=False):
                n = eng.value_load(cnt[0:1, bass.ds(e, 1)], min_val=0, max_val=NS * P)
                gn, en = 17 * l, NE * l

                def tile(q):
                    base = 15 * e + (15 * en + 5 * q)
                    one_hot(o_S, e, q + 1)
                    gated_one_hot(o_Sg, e, q + 1).then_inc(ovf_dve, 1)
                    eng.wait_ge(ovf_pe, base + 1)
                    eng.tensor_copy(hTf[:, 0:512], bank[4][:, :]).then_inc(ovf_dve, 1)
                    eng.wait_ge(ovf_act, 3 * e + (3 * en + q + 1))
                    eng.tensor_tensor(o_act, o_act, bank[5][CAP:2 * CAP, :], ALU.mult).then_inc(ovf_dve, 1)
                    eng.wait_ge(ovf_pe, base + 3)
                    eng.tensor_copy(hTf[:, 1280:1536], bank[7][:, 0:256])
                    eng.tensor_copy(hTf[:, 1024:1280], bank[7][:, 256:512]).then_inc(ovf_dve, 1)
                    eng.wait_ge(ovf_pe, base + 4)
                    eng.tensor_copy(o_y, bank[6][:, :]).then_inc(ovf_dve, 1)

                with eng.If(n > CAP):
                    tile(0)
                    with eng.If(n > 2 * CAP):
                        tile(1)
                        tile(2)
                    with eng.Else():
                        eng.wait_ge(ovf_dve, 15 * e + (15 * en + 5))
                        eng.sem_inc(ovf_dve, 10)
                    eng.nop()
                with eng.Else():
                    eng.sem_inc(ovf_dve, 15)

                eng.wait_ge(gat_done, e + (gn + 1))
                one_hot(S, e + 1, 0).then_inc(S_ready, 1)
                if not first:
                    eng.wait_ge(ST_psum, e + en)
                gated_one_hot(Sg, e, 0).then_inc(Sg_ready, 1)
                eng.wait_ge(silu_done, e + (en + 1))
                eng.tensor_tensor(act, act, bank[5][CAP:2 * CAP, :], ALU.mult).then_inc(act_ready, 1)
                eng.wait_ge(actT_psum, e + (en + 1))
                if not first:
                    eng.wait_ge(down_done, e + en)
                eng.tensor_copy(work[:, 1024:1280], bank[7][:, 256:512]).then_inc(actT_ready, 1)
                if not first:
                    eng.wait_ge(scat_done, e + en)
                eng.tensor_copy(work[:, 1280:1536], bank[7][:, 0:256]).then_inc(ST_ready, 1)

            def moe(l):
                route(l)
                one_hot(S, 0, 0).then_inc(S_ready, 1)
                expert(l, 0, 0, first=True)
                with eng.Fori(0, 5) as it:
                    for j in range(3):
                        expert(l, 3 * it + (j + 1), (j + 1) % 3)

            eng.memset(posm[:, :, :], -1.0)
            eng.memset(gt[:, :, :], 0.0)
            eng.memset(condT[:, :, :], 0.0).then_inc(zeroed, 1)
            eng.wait_ge(attn_in, 16 * 13)
            chain(eng.tensor_tensor(lams[:, 0:128], lams[:, 0:128], lams[:, 128:256], ALU.mult))
            eng.tensor_reduce(lamv[:, 0:2], lams[:, 0:128].rearrange("p (a n) -> p a n", a=2), axis=AX_X,
                              op=ALU.add).then_inc(lam_dots, 1)
            eng.wait_ge(pre_psum, 1)
            eng.tensor_copy(kTs[:, :, 0:P], bank[2][:, :].rearrange("p (h t) -> p h t", h=H)).then_inc(pre_evac, 1)
            eng.wait_ge(pre_psum, 2)
            eng.tensor_copy(work[:, 512:1024], bank[3][:, :]).then_inc(pre_evac, 1)
            norm(0)
            for i in range(4):
                t, s = i // 2, i % 2
                eng.wait_ge(win_evac, i + 1)
                v = qk[:, s, t, :]
                v8 = v.rearrange("p (m d) -> p m d", m=8)
                t8 = tmp.rearrange("p (m d) -> p m d", m=8)
                chain(eng.tensor_tensor(tmp, v, v, ALU.mult))
                chain(eng.tensor_reduce(qss, t8, axis=AX_X, op=ALU.add))
                rstd(qss, DH)
                chain(eng.tensor_tensor(v8, v8, qss.unsqueeze(2).broadcast_to([P, 8, DH]), ALU.mult))
                last = eng.tensor_tensor(v8, v8, (qg, kg)[t].unsqueeze(1).broadcast_to([P, 8, DH]), ALU.mult)
                if s == 1:
                    chain(last)
                    r8 = prob[1][:, 0, 0:2, :].rearrange("p a b -> p (a b)").rearrange("p (m d) -> p m d", m=8)
                    eng.tensor_tensor(t8, v8, col(C_COS, 64).unsqueeze(1).broadcast_to([P, 8, 64]), ALU.mult)
                    for half in range(2):
                        for pt in range(2):
                            o, f = 32 * half + 16 * pt, 32 * half + 16 * (1 - pt)
                            last = eng.tensor_tensor(r8[:, :, o:o + 16], v8[:, :, f:f + 16],
                                                     col(C_SIN + o, 16).unsqueeze(1).broadcast_to([P, 8, 16]), ALU.mult)
                    chain(last)
                    last = eng.tensor_tensor(v8, t8, r8, ALU.add)
                last.then_inc(qk_ready, 1)
                eng.wait_ge(qk_ready, i + 1)
            for g in range(4):
                eng.wait_ge(sg_psum, g // 2 + 1)
                mixed = bank[g // 2][:, 256 * (g % 2):256 * (g % 2) + 256].rearrange("p (s n) -> p s n", s=NS)
                eng.scalar_tensor_tensor(h[:, :, 512 + g * P:512 + (g + 1) * P], mixed, sgbT[:, g:g + 1],
                                         gu[:, :, g * P:(g + 1) * P], ALU.add, ALU.mult).then_inc(sg_used, 1)
            for i, dst in enumerate((qT[:, 0, :, :], kTp)):
                eng.wait_ge(qkT_psum, i + 1)
                eng.tensor_copy(dst, bank[2 + i][:, :].rearrange("p (h t) -> p h t", h=H)).then_inc(qkT_dve, 1)
            for g, (s, b0, heads) in enumerate(((0, 0, 4), (1, 2, 2), (1, 4, 2))):
                eng.wait_ge(score_psum, g + 1)
                h0 = 2 if g == 2 else 0
                for cm in range(2):
                    chain(eng.tensor_reduce(mx[:, s, cm, h0:h0 + heads],
                                            bank[b0 + cm][:, :].rearrange("p (h t) -> p h t", h=heads),
                                            axis=AX_X, op=ALU.max))
                m = mx[:, s, :, h0:h0 + heads]
                eng.tensor_scalar(m, m, -(DH ** -0.5), None, ALU.mult).then_inc(mx_ready, 1)
            eng.wait_ge(lam_exp, 1)
            chain(eng.tensor_tensor(lamv[:, 0:1], lamv[:, 2:3], lamv[:, 3:4], ALU.subtract))
            chain(eng.tensor_scalar(lamv[:, 0:1], lamv[:, 0:1], LAM0, None, ALU.add))
            for s in range(NS):
                eng.wait_ge(exp_ready, 1 + 2 * s)
                es = esum[:, s, :, :]
                chain(eng.reciprocal(es, es))
                chain(eng.tensor_scalar(esum[:, s, 1, :], esum[:, s, 1, :], lamv[:, 0:1], None, ALU.mult))
                for hh in range(H):
                    p0, p1 = prob[s][:, 0, hh, :], prob[s][:, 1, hh, :]
                    chain(eng.tensor_scalar(p1, p1, esum[:, s, 1, hh:hh + 1], None, ALU.mult))
                    eng.scalar_tensor_tensor(p0, p0, esum[:, s, 0, hh:hh + 1], p1, ALU.mult,
                                             ALU.subtract).then_inc(a_map, 1)
            for s in range(NS):
                eng.wait_ge(o_psum, s + 1)
                o = bank[3 + s][:, :]
                hs = h[:, s, 0:512]
                h4 = hs.rearrange("p (h n) -> p h n", h=H)
                chain(eng.tensor_copy(hs, o))
                chain(eng.tensor_tensor(tmp, hs, hs, ALU.mult))
                v = oss[:, 0:4]
                chain(eng.tensor_reduce(v, tmp.rearrange("p (h n) -> p h n", h=H), axis=AX_X, op=ALU.add))
                rstd(v, P)
                chain(eng.tensor_tensor(h4, h4, v.unsqueeze(2).broadcast_to([P, H, P]), ALU.mult))
                eng.scalar_tensor_tensor(h4, h4, 1.0 - LAM0, subg.unsqueeze(1).broadcast_to([P, H, P]),
                                         ALU.mult, ALU.mult).then_inc(att_ready, 1)
            residual(0)
            norm(1)
            moe(0)
            residual(1)
            norm(2)
            residual(2)
            norm(3)
            moe(1)
            residual(3)


_INS = ['x_prompt', 'x_sample', 'cache_k', 'cache_v', 'c', 'c_ctx', 'norm1_g', 'norm2_g', 'w_ada', 'b_ada',
        'w_in', 'w_out', 'q_norm_g', 'k_norm_g', 'lam_q1', 'lam_k1', 'lam_q2', 'lam_k2', 'subln_g',
        'sg_w', 'sg_b', 'pool_w', 'pool_scale', 'router_w', 'router_b', 'w_gate', 'w_up', 'w_down']
_OUTS = [(1, P, D), (1, P, D), (1, 1, P, H, 2, DH), (1, 1, P, H, 2 * DH)]


def kernel(**inputs):
    import numpy as _np
    import concourse.bacc as _bacc
    from concourse import mybir as _mybir
    from concourse.bass_utils import run_bass_kernel_spmd as _run

    nc = _bacc.Bacc("TRN2", target_bir_lowering=False, num_devices=1)
    arrays, args = {}, []
    for name in _INS:
        a = _np.asarray(inputs[name])
        a = _np.ascontiguousarray(a.transpose(0, 2, 1) if name == "sg_b" else a)
        arrays[f"in_{name}_dram"] = a
        args.append(nc.dram_tensor(f"in_{name}_dram", a.shape, _mybir.dt.from_np(a.dtype), kind="ExternalInput").ap())
    t = constant_table()
    arrays["in_table_dram"] = t
    args.append(nc.dram_tensor("in_table_dram", t.shape, _mybir.dt.float32, kind="ExternalInput").ap())
    for i, shape in enumerate(_OUTS):
        args.append(nc.dram_tensor(f"out_{i}_dram", shape, _mybir.dt.float32, kind="ExternalOutput").ap())
    trunk_kernel(nc, *args)
    r = _run(nc, [arrays], core_ids=[0])
    return tuple(r.results[0][f"out_{i}_dram"] for i in range(len(_OUTS)))
```

```python
from contextlib import ExitStack
import math

import numpy as np
import concourse.bass as bass
from concourse import mybir

F32 = mybir.dt.float32
I32 = mybir.dt.int32
BF16 = mybir.dt.bfloat16
ALU = mybir.AluOpType
ACT = mybir.ActivationFunctionType
AX_X = mybir.AxisListType.X

P = 128
D = 1024
KD = D // P
NS = 2
H, DH = 4, 64
NE = 16
FF = 512
KF = FF // P
CAP = 64
NTILE = NS * P // CAP
SLOT = 4096
NSLOT = 9
LAM0 = 0.8 - 0.6 * math.exp(0.0)
EPS = 1e-6
NPART = 3
BIG = 1.0e30
GRID_W = 64
WINDOWS = (2, 4, 8, 16)
SH1, SC1, G1, SH2, SC2, G2 = range(6)

C_ID, C_UP, C_ONE, C_POOL = 0, 128, 256, 384
C_SEL = C_POOL + 4 * P
C_CMP = C_SEL + 2 * P
C_IOTA = C_CMP + NE
C_RANK = C_IOTA + NTILE * CAP
C_COS = C_RANK + 20
C_SIN = C_COS + 64
C_PART = C_SIN + 64
C_N = C_PART + NPART - 1


def constant_table():
    t = np.zeros((P, C_N), np.float32)
    i = np.arange(P)
    t[:, C_ID:C_ID + P] = np.eye(P)
    t[:, C_UP:C_UP + P] = i[:, None] < i[None, :]
    t[:, C_ONE:C_ONE + P] = 1.0
    for g, w in enumerate(WINDOWS):
        lo = np.clip(i - w // 2, 0, P)
        hi = np.clip(i - w // 2 + w, 0, P)
        band = ((i[:, None] >= lo[None, :]) & (i[:, None] < hi[None, :])) / (hi - lo)[None, :].astype(np.float32)
        t[:, C_POOL + g * P:C_POOL + (g + 1) * P] = band - np.eye(P)
    for s in range(NS):
        t[:, C_SEL + s * P:C_SEL + (s + 1) * P] = ((i % 32 < 2 * NPART) & (i % 2 == s))[:, None]
    for part in range(1, NPART):
        t[:, C_PART + part - 1] = -(i % 32 >= 2 * part).astype(np.float32)
    t[:, C_CMP:C_CMP + NE] = (i % 32)[:, None] == np.arange(NE)[None, :]
    t[:, C_IOTA:C_IOTA + NTILE * CAP] = np.arange(NTILE * CAP)
    t[:, C_RANK:C_RANK + 16] = 16 - np.arange(16)
    t[:, C_RANK + 16:C_RANK + 20] = 4 - np.arange(4)
    inv = np.float32(10000.0) ** (-np.arange(16, dtype=np.float32) / 16)
    for half, pos in enumerate((i // GRID_W, i % GRID_W)):
        ang = pos.astype(np.float32)[:, None] * inv[None, :]
        for part, sign in ((0, -1.0), (1, 1.0)):
            c = half * 32 + part * 16
            t[:, C_COS + c:C_COS + c + 16] = np.cos(ang)
            t[:, C_SIN + c:C_SIN + c + 16] = sign * np.sin(ang)
    return t


NPAIR = NE // 2
PAIR_UNITS = 6


def ring_plan():
    filled, last = [0] * NSLOT, [None] * NSLOT
    first = [("ada", 0, 0), ("ada", 1, 1), ("ada", 2, 2), ("ada", 3, 3),
             ("ada", 4, 7), ("ada", 5, 8), ("ada", 6, 0), ("ada", 7, 1), ("win", 0, 2), ("win", 1, 3),
             ("win", 2, 7), ("win", 3, 8), ("win", 4, 0), ("ada", 8, 1), ("wout", 0, 2), ("wout", 1, 3),
             ("ada", 9, 7), ("ada", 10, 8), ("ada", 11, 0)]
    second = [("ada", 12 + i, (7 + i) % NSLOT) for i in range(8)] + [("pool", 0, 6)]
    second += [("ada", 20 + i, (7 + i) % NSLOT) for i in range(4)]
    units, layers = {}, []
    for plan, start in ((first, 4), (second, 2)):
        for kind, u, slot in plan:
            filled[slot] += 1
            units[kind, u] = (slot, filled[slot], last[slot])
            last[slot] = (kind, u)
        layers.append((start, list(filled), list(last)))
        last = [None] * NSLOT
        for n in range(NPAIR * PAIR_UNITS):
            filled[(start + n) % NSLOT] += 1
    return [x[:2] for x in first], [x[:2] for x in second], units, layers


def trunk_kernel(nc, x_prompt, x_sample, cache_k, cache_v, c, c_ctx, norm1_g, norm2_g, w_ada, b_ada,
                 w_in, w_out, q_norm_g, k_norm_g, lam_q1, lam_k1, lam_q2, lam_k2, subln_g,
                 sg_w, sg_b, pool_w, pool_scale, router_w, router_b, w_gate, w_up, w_down, table,
                 y_prompt, y_sample, state_k, state_v):
    first_units, second_units, UNIT, LAYER = ring_plan()

    with ExitStack() as ctx:
        def sb(name, shape, dt=F32):
            return ctx.enter_context(nc.sbuf_tensor(name, shape, dt))

        def sem(name):
            return ctx.enter_context(nc.semaphore(name))

        ring = sb("ring", [P, NSLOT * SLOT])
        x = sb("x", [P, NS, D])
        h = sb("h", [P, NS, D])
        hT = sb("hT", [P, KD, NS * P])
        modp = sb("modp", [P, 3, 512], BF16)
        sel_b = sb("sel_b", [P, NS * P], BF16)
        tab = sb("tab", [P, C_N])
        gam = sb("gam", [P, D])
        bada = sb("bada", [32, 512])
        condT = sb("condT", [P, KD, 32])
        cond = sb("cond", [P, NS, KD])
        rwp = sb("rwp", [P, KD, 32])
        zero_b = sb("zero_b", [P, 512], BF16)
        rb = sb("rb", [P, NE])
        work = sb("work", [P, 3840])
        st = sb("st", [P, 9 * 8])
        rt = sb("rt", [P, 11 * 32 + 48])
        posm = sb("posm", [P, NS, NE + 2])
        gt = sb("gt", [P, NS, NE + 2])
        cnt = sb("cnt", [1, NPAIR], I32)
        vecs = sb("vecs", [P, 2 * 64 + P + 4 + 4])
        bank = [ctx.enter_context(nc.psum_tensor(f"bank{i}", [P, 512], F32)) for i in range(8)]

        def col(a, n):
            return tab[:, a:a + n]

        ident, upper, ones = col(C_ID, P), col(C_UP, P), col(C_ONE, P)

        def slot(i, n=SLOT):
            return ring[:, i * SLOT:i * SLOT + n]

        at = [4 * SLOT]

        def take(n):
            at[0] += n
            assert at[0] <= 7 * SLOT
            return ring[:, at[0] - n:at[0]]

        qk = take(2048).rearrange("p (s t n) -> p s t n", s=NS, t=2)
        vv = take(1024).rearrange("p (s n) -> p s n", s=NS)
        gu = take(1024).rearrange("p (s n) -> p s n", s=NS)
        gv = take(1024).rearrange("p (s n) -> p s n", s=NS)
        ck = take(512)
        cv = take(512)
        qT = take(1024).rearrange("p (s h t) -> p s h t", s=NS, h=H)
        kTp = take(512).rearrange("p (h t) -> p h t", h=H)
        kTs = take(1024).rearrange("p (h t) -> p h t", h=H)
        prob = [take(1024).rearrange("p (c h t) -> p c h t", c=2, h=H),
                take(2048).rearrange("p (c h t) -> p c h t", c=2, h=H)]
        sgw = work[:, 0:512].rearrange("p (g q) -> p g q", g=4)
        sgwT = work[:, 512:1024].rearrange("p (g q) -> p g q", g=4)
        aTp = work[:, 0:512].rearrange("p (h t) -> p h t", h=H)
        aTs = work[:, 1024:2048].rearrange("p (h r t) -> p h r t", h=H, r=2)
        tmp = work[:, 2048:2560]
        xs = work[:, 0:1024]
        xg = work[:, 1024:2048].rearrange("p (k s) -> p k s", k=KD)
        act = work[:, 2048:2560]
        actT = work[:, 2560:3072].rearrange("p (k s) -> p k s", k=KF)
        ysb = work[:, 2048:3072].rearrange("p (q n) -> p q n", q=2)
        STg = work[:, 3072:3328].rearrange("p (s t) -> p s t", s=NS)
        S = work[:, 3328:3584].rearrange("p (s c) -> p s c", s=NS)
        Sg = work[:, 3584:3840].rearrange("p (s c) -> p s c", s=NS)
        gate = work[:, 1024:2048].rearrange("p (q n) -> p q n", q=2)
        rest = work[:, 2048:2560]
        lgT = work[:, 3072:3328]
        rw = work[:, 3072:3200].rearrange("p (k e) -> p k e", k=KD)
        pscale = work[:, 0:1024]
        sq_junk = work[:, 2560:3584]
        hTf = hT[:, :, :].rearrange("p k t -> p (k t)")
        o_xg = hTf[:, 0:1024].rearrange("p (k s) -> p k s", k=KD)
        o_S = hTf[:, 1024:1280].rearrange("p (s c) -> p s c", s=NS)
        o_Sg = hTf[:, 1280:1536].rearrange("p (s c) -> p s c", s=NS)
        lams = work[:, 2560:2816]
        qg, kg, subg = vecs[:, 0:64], vecs[:, 64:128], vecs[:, 128:256]
        lamv, sgbT = vecs[:, 256:260], vecs[:, 260:264]
        ssq = st[:, 0:8]
        qss = st[:, 8:16]
        oss = st[:, 16:24]
        mx = st[:, 24:40].rearrange("p (s c h) -> p s c h", s=NS, c=2)
        esum = st[:, 40:56].rearrange("p (s c h) -> p s c h", s=NS, c=2)

        w_landed = [sem(f"w_landed{i}") for i in range(NSLOT)]
        first_in, attn_in, gam_in, ps_in = sem("first_in"), sem("attn_in"), sem("gam_in"), sem("ps_in")
        sel_ready, mod_first = sem("sel_ready"), sem("mod_first")
        zeroed, cond_ready, lam_dots, lam_exp = sem("zeroed"), sem("cond_ready"), sem("lam_dots"), sem("lam_exp")
        ada_done, pool_done = sem("ada_done"), sem("pool_done")
        mod_ready, tab_in, x_in = sem("mod_ready"), sem("tab_in"), sem("x_in")
        ss_ready, sc_ready, sc_used = sem("ss_ready"), sem("sc_ready"), sem("sc_used")
        sh_ready, h_ready, rw_ready = sem("sh_ready"), sem("h_ready"), sem("rw_ready")
        gam_used = sem("gam_used")
        tr_psum, tr_done = sem("tr_psum"), sem("tr_done")
        pre_psum, pre_evac = sem("pre_psum"), sem("pre_evac")
        win_psum, win_evac, qk_ready = sem("win_psum"), sem("win_evac"), sem("qk_ready")
        qkT_psum, qkT_dve, qkT_act = sem("qkT_psum"), sem("qkT_dve"), sem("qkT_act")
        sg_psum, sg_used = sem("sg_psum"), sem("sg_used")
        score_psum, mx_ready, exp_ready, a_map = sem("score_psum"), sem("mx_ready"), sem("exp_ready"), sem("a_map")
        aT_psum, aT_sb, o_psum, att_ready = sem("aT_psum"), sem("aT_sb"), sem("o_psum"), sem("att_ready")
        oss_ready = sem("oss_ready")
        res_ready, gate_sb, res_used, x_ready = sem("res_ready"), sem("gate_sb"), sem("res_used"), sem("x_ready")
        lgT_psum, lgT_sb = sem("lgT_psum"), sem("lgT_sb")
        logit_psum, router_exp, chosen, pos_psum, routed = (sem("logit_psum"), sem("router_exp"),
                                                            sem("chosen"), sem("pos_psum"), sem("routed"))
        dT_psum, dT_sb = sem("dT_psum"), sem("dT_sb")
        S_ready, Sg_half, Sg_ready, gat_done = sem("S_ready"), sem("Sg_half"), sem("Sg_ready"), sem("gat_done")
        xs_ready, xgT_psum, xg_act, xg_dve = sem("xs_ready"), sem("xgT_psum"), sem("xg_act"), sem("xg_dve")
        gate_done, up_done, silu_done, act_ready = sem("gate_done"), sem("up_done"), sem("silu_done"), sem("act_ready")
        actT_psum, actT_ready, ST_ready = sem("actT_psum"), sem("actT_ready"), sem("ST_ready")
        down_half = sem("down_half")
        down_done, y_act, y_dve, scat_done = sem("down_done"), sem("y_act"), sem("y_dve"), sem("scat_done")
        ovf_pe, ovf_act, ovf_dve = sem("ovf_pe"), sem("ovf_act"), sem("ovf_dve")
        dve_step = sem("dve_step")
        state_out, y_out = sem("state_out"), sem("y_out")

        block = ctx.enter_context(nc.Block())

        def expert_weights(w, l, e, n):
            flat = w.rearrange("l e (p k) f -> (l e) p (k f)", k=n)
            return flat[bass.ds(NE * l + e, 1), :, :].rearrange("a p n -> p (a n)")

        ada_v = w_ada.rearrange("l (p k) n -> l p k n", k=KD)
        win_v = w_in[0].rearrange("(p k) n -> p k n", k=KD)
        wout_v = w_out[0].rearrange("(p k) n -> p k n", k=KD)
        pool_v = pool_w[0].rearrange("g (j p) n -> p (g j) n", p=P)

        @block.sync
        def _(eng):
            def wait_used(name):
                kind, u = name
                if kind == "ada":
                    eng.wait_ge(ada_done, u // 4 + 1)
                elif kind == "win":
                    eng.wait_ge(win_psum, 2 * u + 2)
                elif kind == "wout":
                    eng.wait_ge(res_ready, u + 3)
                else:
                    eng.wait_ge(pool_done, 1)

            def unit(name):
                i, _, before = UNIT[name]
                kind, u = name
                if before:
                    wait_used(before)
                if kind == "pool":
                    dst = slot(i, 2048).rearrange("p (m n) -> p m n", m=8)
                    eng.dma_start(dst, pool_v).then_inc(w_landed[i], 16)
                    return
                src = {"ada": lambda: ada_v[u // 12, :, :, 512 * (u % 12):512 * (u % 12) + 512],
                       "win": lambda: win_v[:, :, 512 * u:512 * u + 512],
                       "wout": lambda: wout_v[:, :, 512 * u:512 * u + 512]}[kind]()
                eng.dma_start(slot(i).rearrange("p (k n) -> p k n", k=KD), src).then_inc(w_landed[i], 16)

            def wait_expert_unit(l, n, it):
                done = (gate_done, up_done, down_done)[n % PAIR_UNITS // 2]
                eng.wait_ge(done, 3 * it + (NPAIR * l + n // PAIR_UNITS + 1))

            def load_pair(l, p, it):
                start, _, last_unit = LAYER[l]
                for j in range(PAIR_UNITS):
                    n = PAIR_UNITS * p + j
                    i = (start + n) % NSLOT
                    if n >= NSLOT:
                        wait_expert_unit(l, n - NSLOT, it)
                    elif last_unit[i]:
                        wait_used(last_unit[i])
                    elif l == 0 and i == 4:
                        eng.wait_ge(att_ready, 2)
                        eng.wait_ge(o_psum, 2)
                        eng.wait_ge(state_out, 32)
                    w, k = ((w_gate, KD), (w_up, KD), (w_down, KF))[j // 2]
                    eng.dma_start(slot(i), expert_weights(w, l, 6 * it + (2 * p + j % 2), k)).then_inc(w_landed[i], 16)

            for dst, src in ((cond[:, 0, :], c_ctx.rearrange("(p k) -> p k", k=KD)),
                             (cond[:, 1, :], c[0].rearrange("(p k) -> p k", k=KD)),
                             (bada[0:24, :], b_ada.rearrange("l (u n) -> (l u) n", n=512)),
                             (bada[24:32, :], b_ada[0].rearrange("(u n) -> u n", n=512)[0:8, :])):
                eng.dma_start(dst, src).then_inc(first_in, 16)
            eng.dma_start(tab[:, :], table[:, :]).then_inc(tab_in, 16)
            for name in first_units:
                unit(name)
                if name == ("ada", 3):
                    eng.dma_start(x[:, 0, :], x_prompt[0]).then_inc(x_in, 16)
                    eng.dma_start(x[:, 1, :], x_sample[0]).then_inc(x_in, 16)
            for l in range(2):
                load_pair(l, 0, 0)
                load_pair(l, 1, 0)
                with eng.Fori(0, 2) as it:
                    for p in range(2, 5):
                        load_pair(l, p, it)
                if l == 0:
                    for n, name in enumerate(second_units):
                        if n < NSLOT:
                            wait_expert_unit(0, NPAIR * PAIR_UNITS - NSLOT + n, 0)
                        unit(name)
            for s, y in enumerate((y_prompt, y_sample)):
                eng.wait_ge(x_ready, 7 + s)
                eng.dma_start(y[0], x[:, s, :]).then_inc(y_out, 16)
            eng.wait_ge(y_out, 32)

        @block.gpsimd
        def _(eng):
            eng.wait_ge(qk_ready, 3)
            eng.dma_start(state_k[0, 0].rearrange("t h c d -> t (h c d)"), qk[:, 0, 1, :]).then_inc(state_out, 16)
            eng.wait_ge(win_evac, 5)
            eng.dma_start(state_v[0, 0].rearrange("t h d -> t (h d)"), vv[:, 0, :]).then_inc(state_out, 16)
            eng.wait_ge(state_out, 32)

        def mod_unit(j, hf):
            return 2 * j + hf

        @block.tensor
        def _(eng):
            mm = nc.tensor.matmul

            def ada_batch(b, chunks=range(KD)):
                if b >= 2:
                    eng.wait_ge(mod_ready, b - 1)
                ws = []
                for g in range(4):
                    i, fill, _ = UNIT["ada", 4 * b + g]
                    eng.wait_ge(w_landed[i], 16 * fill)
                    ws.append(slot(i).rearrange("p (k n) -> p k n", k=KD))
                out = bank[6 + b % 2]
                for k in chunks:
                    for g in range(4):
                        mm(out[32 * g:32 * g + 32, :], condT[:, k, :], ws[g][:, k, :],
                           start=k == 0, stop=False, skip_group_check=True)
                if KD - 1 not in chunks:
                    return
                for g in range(4):
                    a = 4 * b + g
                    last = mm(out[32 * g:32 * g + 2 * NPART, :],
                              ident[0:32, a:a + 1].broadcast_to([32, 2 * NPART]), bada[:, :],
                              start=False, stop=True, skip_group_check=True)
                last.then_inc(ada_done, 1)

            def broadcast_mod(out, l, j, hf, s):
                u = mod_unit(j, hf)
                g = u % 4
                eng.wait_ge(mod_ready, 3 * l + u // 4 + 1)
                return mm(out, sel_b[32 * g:32 * g + 32, s * P:(s + 1) * P],
                          modp[32 * g:32 * g + 32, u // 4 % 3, :], start=True, stop=True)

            def norm_scales(n):
                for cc in range(4):
                    if cc >= 2:
                        eng.wait_ge(sc_used, 4 * n + cc - 1)
                    broadcast_mod(bank[6 + cc % 2][:, :], n // 2, 3 * (n % 2) + 1, cc % 2,
                                  cc // 2).then_inc(sc_ready, 1)

            def norm_shifts(n):
                for cc in range(4):
                    broadcast_mod(bank[cc][:, :], n // 2, 3 * (n % 2), cc % 2, cc // 2).then_inc(sh_ready, 1)

            def transpose_rows(cidx, wait_source):
                for ii in range(4 * cidx, 4 * cidx + 4):
                    s, j = (ii % 4) // 2, ii % 2
                    wait_source(s)
                    if ii >= 2:
                        eng.wait_ge(tr_done, ii - 1)
                    for kk in range(4):
                        last = nc.tensor.transpose(bank[4 + j][:, kk * P:(kk + 1) * P],
                                                   h[:, s, 4 * j + kk::KD], ident)
                    last.then_inc(tr_psum, 1)

            def residual_gates(r, l, j):
                for ri in range(4 * r, 4 * r + 4):
                    if ri % 4 >= 2:
                        eng.wait_ge(gate_sb, ri - 1)
                    broadcast_mod(bank[4 + ri % 2][:, :], l, j, ri % 2, (ri % 4) // 2).then_inc(res_ready, 1)

            def route(l):
                eng.wait_ge(mod_ready, 3 * (l + 1))
                eng.wait_ge(sc_used, 4 * (2 * l + 2))
                eng.wait_ge(tr_done, 12 + 4 * l)
                eng.wait_ge(rw_ready, 1)
                for k in range(KD):
                    g = k % 4
                    last = mm(bank[7][32 * g:32 * g + 32, 0:NS * P], rwp[:, k, :], hT[:, k, :],
                              start=k < 4, stop=k >= 4, skip_group_check=True)
                last.then_inc(lgT_psum, 1)
                eng.wait_ge(lgT_sb, l + 1)
                for s in range(NS):
                    last = mm(bank[6][:, s * NE:(s + 1) * NE], lgT[:, s * P:(s + 1) * P], col(C_CMP, NE),
                              start=True, stop=True)
                last.then_inc(logit_psum, 1)
                for b in range(4):
                    mm(bank[b][:, :], zero_b[:, 0:P], zero_b[:, :], start=True, stop=False, skip_group_check=True)
                eng.wait_ge(chosen, l + 1)
                m0, m1 = [rt[:, 320 + s * NE:320 + (s + 1) * NE] for s in range(NS)]
                mm(bank[6][:, 64:80], upper, m0, start=True, stop=True)
                mm(bank[6][:, 80:96], ones, m0, start=True, stop=False)
                mm(bank[6][:, 80:96], upper, m1, start=False, stop=True)
                mm(bank[6][:, 96:112], ones, m0, start=True, stop=False)
                mm(bank[6][:, 96:112], ones, m1, start=False, stop=True).then_inc(pos_psum, 1)

            def gather(src, q):
                for s in range(NS):
                    last = mm(bank[6 + q][:, :], src[:, s, :], h[:, s, 512 * q:512 * q + 512],
                              start=s == 0, stop=s == NS - 1)
                return last

            def gathered_transposes():
                for k in range(KD):
                    last = nc.tensor.transpose(bank[4 + k // 4][:, (k % 4) * P:(k % 4 + 1) * P], xs[:, k::KD], ident)
                return last

            def side_by_side(out, lhs, wa, wb, nk):
                for k in range(nk):
                    for q, w in enumerate((wa, wb)):
                        last = mm(out[CAP * q:CAP * (q + 1), :], lhs[:, k, CAP * q:CAP * (q + 1)], w(k),
                                  start=k == 0, stop=k == nk - 1, skip_group_check=True)
                return last

            def project(out, lhs, slots):
                v = [slot(i).rearrange("p (k f) -> p k f", k=KD) for i in slots]
                return side_by_side(out, lhs, lambda k: v[0][:, k, :], lambda k: v[1][:, k, :], KD)

            def down(slots, q):
                v = [slot(i).rearrange("p (k d) -> p k d", k=KF) for i in slots]
                cs = slice(512 * q, 512 * q + 512)
                return side_by_side(bank[6 + q], actT, lambda k: v[0][:, k, cs], lambda k: v[1][:, k, cs], KF)

            def activation_transposes():
                for k in range(KF):
                    last = nc.tensor.transpose(bank[4][:, k * P:(k + 1) * P], act[:, k::KF], ident)
                return last

            def scatter_transposes(sg):
                for s in range(NS):
                    last = nc.tensor.transpose(bank[5][:, s * P:(s + 1) * P], sg[:, s, :], ident)
                return last

            def scatter():
                for s in range(NS):
                    for q in range(2):
                        last = mm(bank[2 * s + q][:, :], STg[:, s, :], ysb[:, q, :], start=False, stop=False,
                                  skip_group_check=True)
                return last

            def pair(l, p, it=None):
                start, filled, _ = LAYER[l]
                ln = NPAIR * l
                t = 0 if it is None else 3 * it
                first = it is None and p == 0
                slots, landed = [], []
                for j in range(PAIR_UNITS):
                    n = PAIR_UNITS * p + j
                    i = (start + n) % NSLOT
                    slots.append(i)
                    fills = filled[i] + 1 + sum((start + m) % NSLOT == i for m in range(n))
                    landed.append(16 * fills if it is None else 32 * it + 16 * fills)

                def wait_unit(*js):
                    for j in js:
                        eng.wait_ge(w_landed[slots[j]], landed[j])

                def tile(q):
                    base = 18 * (ln + p) + 6 * q + (0 if it is None else 54 * it)
                    eng.wait_ge(ovf_dve, base + 1)
                    gather(o_S, 0)
                    gather(o_S, 1).then_inc(ovf_pe, 1)
                    eng.wait_ge(ovf_dve, base + 2)
                    gathered_transposes().then_inc(ovf_pe, 1)
                    eng.wait_ge(ovf_dve, base + 3)
                    project(bank[4], o_xg, slots[0:2])
                    project(bank[5], o_xg, slots[2:4]).then_inc(ovf_pe, 1)
                    eng.wait_ge(ovf_dve, base + 4)
                    activation_transposes()
                    scatter_transposes(o_Sg).then_inc(ovf_pe, 1)
                    eng.wait_ge(ovf_dve, base + 5)
                    down(slots[4:6], 0)
                    down(slots[4:6], 1).then_inc(ovf_pe, 1)
                    eng.wait_ge(ovf_dve, base + 6)
                    scatter().then_inc(ovf_pe, 1)

                n = eng.value_load(cnt[0:1, bass.ds(t + p, 1)], min_val=0, max_val=NS * P)
                eng.wait_ge(xg_act, t + (9 * l + p + 1))
                eng.wait_ge(xg_dve, t + (9 * l + p + 1))
                with eng.If(n > CAP):
                    wait_unit(*range(PAIR_UNITS))
                    tile(0)
                    with eng.If(n > 2 * CAP):
                        tile(1)
                        tile(2)
                    with eng.Else():
                        eng.wait_ge(ovf_pe, 18 * (ln + p) + 6 + (0 if it is None else 54 * it))
                        eng.sem_inc(ovf_pe, 12)
                    eng.nop()
                with eng.Else():
                    eng.sem_inc(ovf_pe, 18)

                wait_unit(0, 1)
                project(bank[4], xg, slots[0:2]).then_inc(gate_done, 1)
                wait_unit(2, 3)
                project(bank[5], xg, slots[2:4]).then_inc(up_done, 1)
                eng.wait_ge(S_ready, t + (9 * l + p + 2))
                gather(S, 0).then_inc(gat_done, 1)
                eng.wait_ge(Sg_ready, t + (ln + p + 1))
                eng.wait_ge(act_ready, t + (ln + p + 1))
                activation_transposes().then_inc(actT_psum, 1)
                scatter_transposes(Sg).then_inc(actT_psum, 1)
                gather(S, 1).then_inc(gat_done, 1)
                wait_unit(4, 5)
                eng.wait_ge(actT_ready, t + (ln + p + 1))
                eng.wait_ge(xs_ready, 2 * t + (2 * (9 * l + p + 2) - 1))
                down(slots[4:6], 0).then_inc(down_half, 1)
                eng.wait_ge(xs_ready, 2 * t + 2 * (9 * l + p + 2))
                down(slots[4:6], 1).then_inc(down_done, 1)
                eng.wait_ge(ST_ready, t + (ln + p + 1))
                gathered_transposes().then_inc(xgT_psum, 1)
                eng.wait_ge(y_act, t + (ln + p + 1))
                eng.wait_ge(y_dve, t + (ln + p + 1))
                scatter().then_inc(scat_done, 1)

            def moe(l):
                eng.wait_ge(routed, l + 1)
                eng.wait_ge(S_ready, 9 * l + 1)
                gather(S, 0).then_inc(gat_done, 1)
                gather(S, 1).then_inc(gat_done, 1)
                eng.wait_ge(xs_ready, 2 * (9 * l + 1))
                gathered_transposes().then_inc(xgT_psum, 1)
                pair(l, 0)
                pair(l, 1)
                with eng.Fori(0, 2) as it:
                    for p in range(2, 5):
                        pair(l, p, it)
                eng.wait_ge(xg_act, 9 * (l + 1))
                eng.wait_ge(xg_dve, 9 * (l + 1))

            eng.wait_ge(tab_in, 16)
            eng.wait_ge(cond_ready, NPART)
            ada_batch(0)
            eng.wait_ge(sel_ready, 1)
            norm_scales(0)
            norm_shifts(0)
            eng.wait_ge(attn_in, 16 * 13)
            for i, src in enumerate((ck.rearrange("p (h t) -> p h t", h=H), sgw)):
                for k in range(4):
                    last = nc.tensor.transpose(bank[4 + i][:, k * P:(k + 1) * P], src[:, k, :], ident)
                last.then_inc(pre_psum, 1)
            eng.wait_ge(pre_evac, 2)
            transpose_rows(0, lambda s: eng.wait_ge(h_ready, 2 * s + 2))
            ada_batch(1)
            for i in range(10):
                u, s = i // 2, i % 2
                sl, fill, _ = UNIT[("win", u)]
                eng.wait_ge(w_landed[sl], 16 * fill)
                eng.wait_ge(tr_done, 2 * s + 2)
                if i >= 2:
                    eng.wait_ge(win_evac, i - 1)
                w = slot(sl).rearrange("p (k n) -> p k n", k=KD)
                for k in range(KD):
                    last = mm(bank[i % 2][:, :], hT[:, k, s * P:(s + 1) * P], w[:, k, :],
                              start=k == 0, stop=k == KD - 1)
                last.then_inc(win_psum, 1)
            eng.wait_ge(win_evac, 10)
            for g in range(4):
                last = mm(bank[g // 2][:, 256 * (g % 2):256 * (g % 2) + 256].rearrange("p (s n) -> p s n", s=NS),
                          sgwT[:, g, :], gv[:, :, g * P:(g + 1) * P], start=True, stop=True)
                if g % 2:
                    last.then_inc(sg_psum, 1)
            for i in range(4):
                s, t = i // 2, i % 2
                eng.wait_ge(qk_ready, (1, 3, 2, 4)[i])
                for hh in range(H):
                    last = nc.tensor.transpose(bank[2 + i][:, hh * P:(hh + 1) * P],
                                               qk[:, s, t, hh * P:(hh + 1) * P], ident)
                last.then_inc(qkT_psum, 1)

            def score(b, s, cmap, heads):
                keys, n = (kTp, P) if s == 0 else (kTs, 2 * P)
                r = slice(64 * cmap, 64 * cmap + 64)
                for q, hh in enumerate(heads):
                    last = mm(bank[b][:, q * n:(q + 1) * n], qT[r, s, hh, :], keys[r, hh, :], start=True, stop=True)
                return last

            eng.wait_ge(sg_used, 4)
            eng.wait_ge(qkT_dve, 2)
            score(0, 0, 0, range(4))
            score(1, 0, 1, range(4)).then_inc(score_psum, 1)
            eng.wait_ge(qkT_act, 2)
            for hp in range(2):
                score(2 + 2 * hp, 1, 0, (2 * hp, 2 * hp + 1))
                score(3 + 2 * hp, 1, 1, (2 * hp, 2 * hp + 1)).then_inc(score_psum, 1)
            ada_batch(2, range(4))
            eng.wait_ge(a_map, 4)
            for hh in range(H):
                last = nc.tensor.transpose(bank[0][:, hh * P:(hh + 1) * P], prob[0][:, 0, hh, :], ident)
            last.then_inc(aT_psum, 1)
            for hp in range(2):
                eng.wait_ge(a_map, 6 + 2 * hp)
                for q in range(4):
                    last = nc.tensor.transpose(bank[1 + hp][:, q * P:(q + 1) * P],
                                               prob[1][:, 0, 2 * hp + q // 2, (q % 2) * P:(q % 2 + 1) * P], ident)
                last.then_inc(aT_psum, 1)
            eng.wait_ge(aT_sb, 1)
            for hh in range(H):
                last = mm(bank[3][:, hh * P:(hh + 1) * P], aTp[:, hh, :], vv[:, 0, hh * P:(hh + 1) * P],
                          start=True, stop=True)
            last.then_inc(o_psum, 1)
            eng.wait_ge(aT_sb, 3)
            for hh in range(H):
                o = bank[4][:, hh * P:(hh + 1) * P]
                mm(o, aTs[:, hh, 0, :], cv[:, hh * P:(hh + 1) * P], start=True, stop=False)
                last = mm(o, aTs[:, hh, 1, :], vv[:, 1, hh * P:(hh + 1) * P], start=False, stop=True)
            last.then_inc(o_psum, 1)
            ada_batch(2, range(4, KD))
            eng.wait_ge(att_ready, 2)
            transpose_rows(1, lambda s: None)
            for ri in range(4):
                s, u = ri // 2, ri % 2
                sl, fill, _ = UNIT[("wout", u)]
                eng.wait_ge(w_landed[sl], 16 * fill)
                eng.wait_ge(tr_done, 6 + 2 * s)
                w = slot(sl).rearrange("p (k n) -> p k n", k=KD)
                for k in range(KD):
                    last = mm(bank[ri][:, :], hT[:, k, s * P:(s + 1) * P], w[:, k, :],
                              start=k == 0, stop=k == KD - 1)
                eng.wait_ge(tr_done, 8)
                if ri >= 2:
                    eng.wait_ge(gate_sb, ri - 1)
                broadcast_mod(bank[4 + ri % 2][:, :], 0, G1, u, s).then_inc(res_ready, 1)
            norm_scales(1)
            eng.wait_ge(res_used, 4)
            norm_shifts(1)
            transpose_rows(2, lambda s: eng.wait_ge(h_ready, 4 + 2 * s + 2))
            route(0)
            moe(0)
            residual_gates(1, 0, G2)

            ada_batch(3)
            norm_scales(2)
            eng.wait_ge(res_used, 8)
            norm_shifts(2)
            sl, fill, _ = UNIT["pool", 0]
            pw = slot(sl, 2048).rearrange("p (g j n) -> p g j n", g=4, j=2)
            for s in range(NS):
                eng.wait_ge(h_ready, 8 + 2 * s + 2)
                for j in range(2):
                    for kk in range(4):
                        ch = 4 * j + kk
                        last = mm(bank[4 + j][:, kk * P:(kk + 1) * P], h[:, s, ch * P:(ch + 1) * P],
                                  col(C_POOL + (ch // 2) * P, P), start=True, stop=True)
                    last.then_inc(dT_psum, 1)
                if s == 0:
                    eng.wait_ge(dT_sb, 2)
            ada_batch(4)
            eng.wait_ge(w_landed[sl], 16 * fill)
            for s in range(NS):
                eng.wait_ge(dT_sb, 2 * s + 2)
                for g in range(4):
                    for j in range(2):
                        last = mm(bank[2 * s + g // 2][:, 256 * (g % 2):256 * (g % 2) + 256],
                                  hT[:, 2 * g + j, s * P:(s + 1) * P], pw[:, g, j, :], start=j == 0, stop=j == 1)
            last.then_inc(pool_done, 1)
            residual_gates(2, 1, G1)
            ada_batch(5)
            norm_scales(3)
            eng.wait_ge(res_used, 12)
            norm_shifts(3)
            transpose_rows(3, lambda s: eng.wait_ge(h_ready, 12 + 2 * s + 2))
            route(1)
            moe(1)
            residual_gates(3, 1, G2)

        @block.scalar
        def _(eng):
            eng.dma_start(gam[:, :], norm1_g[0:1, :].broadcast_to([P, D])).then_inc(gam_in, 16)
            for dst, src in ((ck, cache_k[0, 0].rearrange("t h c d -> t (h c d)")),
                             (cv, cache_v[0, 0].rearrange("t h d -> t (h d)")),
                             (sgw, sg_w[0].rearrange("g p q -> p g q")),
                             (qg, q_norm_g[0:1, :].broadcast_to([P, 64])),
                             (kg, k_norm_g[0:1, :].broadcast_to([P, 64])),
                             (lams[:, 0:64], lam_q1[0:1, :].broadcast_to([P, 64])),
                             (lams[:, 64:128], lam_q2[0:1, :].broadcast_to([P, 64])),
                             (lams[:, 128:192], lam_k1[0:1, :].broadcast_to([P, 64])),
                             (lams[:, 192:256], lam_k2[0:1, :].broadcast_to([P, 64])),
                             (subg, subln_g[0:1, :].broadcast_to([P, P])),
                             (sgbT, sg_b[0]),
                             (rb[:, :], router_b.rearrange("(a n) -> a n", a=1).broadcast_to([P, NE])),
                             (rw[:, :, :], router_w.rearrange("(p k) e -> p k e", k=KD))):
                eng.dma_start(dst, src).then_inc(attn_in, 16)

            def evac(dst, b, cols=slice(0, 512)):
                return eng.activation(dst, b[:, cols], ACT.Copy)

            def evac_mod(b):
                eng.wait_ge(ada_done, b + 1)
                evac(modp[:, b % 3, :], bank[6 + b % 2]).then_inc(mod_first, 1)

            def squares(n):
                for s in range(NS):
                    if n:
                        eng.wait_ge(x_ready, 2 * (n - 1) + s + 1)
                    eng.activation(hTf[:, s * D:(s + 1) * D], x[:, s, :], ACT.Square,
                                   accum_out=ssq[:, 2 * n + s:2 * n + s + 1]).then_inc(ss_ready, 1)

            def evac_gates(r):
                for ri in range(4 * r, 4 * r + 4):
                    eng.wait_ge(res_ready, ri + 1)
                    if ri % 4 >= 2:
                        eng.wait_ge(res_used, ri - 1)
                    evac(gate[:, ri % 2, :], bank[4 + ri % 2]).then_inc(gate_sb, 1)

            def evac_transposes(cidx):
                for ii in range(4 * cidx, 4 * cidx + 4):
                    s, j = (ii % 4) // 2, ii % 2
                    eng.wait_ge(tr_psum, ii + 1)
                    eng.activation(hT[:, 4 * j:4 * j + 4, s * P:(s + 1) * P],
                                   bank[4 + j][:, :].rearrange("p (k t) -> p k t", k=4),
                                   ACT.Copy).then_inc(tr_done, 1)

            def pair(l, p, it=None):
                ln = NPAIR * l
                t = 0 if it is None else 3 * it
                n = eng.value_load(cnt[0:1, bass.ds(t + p, 1)], min_val=0, max_val=NS * P)

                def tile(q):
                    eng.wait_ge(ovf_pe, 18 * (ln + p) + 6 * q + 3 + (0 if it is None else 54 * it))
                    eng.activation(act, bank[4][:, :], ACT.Silu).then_inc(ovf_act, 1)

                with eng.If(n > CAP):
                    tile(0)
                    with eng.If(n > 2 * CAP):
                        tile(1)
                        tile(2)
                    with eng.Else():
                        eng.wait_ge(ovf_act, 3 * (ln + p) + 1 + (0 if it is None else 9 * it))
                        eng.sem_inc(ovf_act, 2)
                    eng.nop()
                with eng.Else():
                    eng.sem_inc(ovf_act, 3)

                eng.wait_ge(gate_done, t + (ln + p + 1))
                eng.activation(act, bank[4][:, :], ACT.Silu).then_inc(silu_done, 1)
                for q in range(2):
                    eng.wait_ge(gat_done, 2 * t + (2 * (9 * l + p + 1) + q + 1))
                    evac(xs[:, 512 * q:512 * q + 512], bank[6 + q]).then_inc(xs_ready, 1)
                eng.wait_ge(down_half, t + (ln + p + 1))
                evac(ysb[:, 0, :], bank[6]).then_inc(y_act, 1)
                eng.wait_ge(xgT_psum, t + (9 * l + p + 2))
                evac(work[:, 1024:1536], bank[4]).then_inc(xg_act, 1)

            def moe(l):
                eng.wait_ge(logit_psum, l + 1)
                eng.activation(rt[:, 0:32], bank[6][:, 0:32], ACT.Exp, scale=-1.0).then_inc(router_exp, 1)
                for q in range(2):
                    eng.wait_ge(gat_done, 2 * 9 * l + q + 1)
                    evac(xs[:, 512 * q:512 * q + 512], bank[6 + q]).then_inc(xs_ready, 1)
                eng.wait_ge(xgT_psum, 9 * l + 1)
                evac(work[:, 1024:1536], bank[4]).then_inc(xg_act, 1)
                eng.wait_ge(routed, l + 1)
                pair(l, 0)
                pair(l, 1)
                with eng.Fori(0, 2) as it:
                    for p in range(2, 5):
                        pair(l, p, it)

            def load_gamma(v, used):
                eng.wait_ge(gam_used, used)
                eng.dma_start(gam[:, :], v.broadcast_to([P, D])).then_inc(gam_in, 16)

            eng.wait_ge(first_in, 16 * 4)
            eng.wait_ge(zeroed, 1)
            for i in range(NPART):
                eng.activation(condT[:, :, NS * i:NS * (i + 1)].rearrange("p k s -> p s k"), cond[:, :, :],
                               ACT.Silu).then_inc(cond_ready, 1)
            eng.wait_ge(x_in, 32)
            squares(0)
            evac_mod(0)
            evac_transposes(0)
            evac_mod(1)
            for i in range(10):
                u, s = i // 2, i % 2
                eng.wait_ge(win_psum, i + 1)
                dst = (qk[:, s, 0, :], qk[:, s, 1, :], vv[:, s, :], gu[:, s, :], gv[:, s, :])[u]
                eng.activation(dst, bank[i % 2][:, :], ACT.Copy if u < 3 else ACT.Gelu_apprx_tanh).then_inc(win_evac, 1)
            load_gamma(norm2_g[0:1, :], 1)
            for i in (2, 3):
                eng.wait_ge(qkT_psum, i + 1)
                dst = qT[:, 1, :, :] if i == 2 else kTs[:, :, P:2 * P]
                eng.activation(dst, bank[2 + i][:, :].rearrange("p (h t) -> p h t", h=H), ACT.Copy).then_inc(qkT_act, 1)
            eng.wait_ge(lam_dots, 1)
            eng.activation(lamv[:, 2:4], lamv[:, 0:2], ACT.Exp).then_inc(lam_exp, 1)
            for g, (s, b0, heads) in enumerate(((0, 0, range(4)), (1, 2, (0, 1)), (1, 4, (2, 3)))):
                n = P if s == 0 else 2 * P
                eng.wait_ge(mx_ready, g + 1)
                for cm in range(2):
                    for q, hh in enumerate(heads):
                        last = eng.activation(prob[s][:, cm, hh, :], bank[b0 + cm][:, q * n:(q + 1) * n], ACT.Exp,
                                              bias=mx[:, s, cm, hh:hh + 1], scale=DH ** -0.5,
                                              accum_out=esum[:, s, cm, hh:hh + 1])
                last.then_inc(exp_ready, 1)
            for i, dst in enumerate((work[:, 0:512], work[:, 1024:1536], work[:, 1536:2048])):
                eng.wait_ge(aT_psum, i + 1)
                evac(dst, bank[i]).then_inc(aT_sb, 1)
            for s in range(NS):
                eng.wait_ge(o_psum, s + 1)
                for hh in range(H):
                    last = eng.activation(sq_junk[:, (H * s + hh) * P:(H * s + hh + 1) * P],
                                          bank[3 + s][:, hh * P:(hh + 1) * P], ACT.Square,
                                          accum_out=oss[:, H * s + hh:H * s + hh + 1])
                last.then_inc(oss_ready, 1)
            evac_mod(2)
            evac_transposes(1)
            evac_gates(0)
            squares(1)
            evac_transposes(2)
            load_gamma(norm1_g[1:2, :], 2)
            moe(0)
            eng.wait_ge(scat_done, NPAIR)
            eng.dma_start(pscale, pool_scale[0:1, :].broadcast_to([P, D])).then_inc(ps_in, 16)
            eng.wait_ge(xg_dve, 9)
            evac_gates(1)
            squares(2)
            evac_mod(3)
            for ii in range(4):
                s, j = ii // 2, ii % 2
                eng.wait_ge(dT_psum, ii + 1)
                eng.activation(hT[:, 4 * j:4 * j + 4, s * P:(s + 1) * P],
                               bank[4 + j][:, :].rearrange("p (k t) -> p k t", k=4), ACT.Copy).then_inc(dT_sb, 1)
            load_gamma(norm2_g[1:2, :], 3)
            evac_mod(4)
            evac_gates(2)
            squares(3)
            evac_mod(5)
            evac_transposes(3)
            moe(1)
            eng.wait_ge(xg_dve, 18)
            evac_gates(3)

        @block.vector
        def _(eng):
            steps = [0]

            def chain(ins):
                steps[0] += 1
                ins.then_inc(dve_step, 1)
                eng.wait_ge(dve_step, steps[0])

            def rstd(v, n):
                w = v.shape[1]
                y, t = st[:, 56:56 + w], st[:, 64:64 + w]
                chain(eng.tensor_scalar(v, v, 1.0 / n, EPS, ALU.mult, ALU.add))
                chain(eng.tensor_scalar(t.bitcast(I32), v.bitcast(I32), 1, None, ALU.logical_shift_right))
                chain(eng.tensor_scalar(y.bitcast(I32), t.bitcast(I32), -1.0, float(0x5f3759df), ALU.mult, ALU.add))
                for i in range(3):
                    chain(eng.tensor_tensor(t, y, y, ALU.mult))
                    chain(eng.scalar_tensor_tensor(t, t, -0.5, v, ALU.mult, ALU.mult))
                    chain(eng.scalar_tensor_tensor(v if i == 2 else y, t, 1.5, y, ALU.add, ALU.mult))

            def split(b):
                eng.wait_ge(mod_first, b + 1)
                v, part = bank[6 + b % 2][:, :], modp[:, b % 3, :]
                chain(eng.scalar_tensor_tensor(rest, part, col(C_PART, 1), v, ALU.mult, ALU.add))
                chain(eng.tensor_copy(part, rest))
                eng.scalar_tensor_tensor(part, part, col(C_PART + 1, 1), rest, ALU.mult,
                                         ALU.add).then_inc(mod_ready, 1)
                eng.wait_ge(mod_ready, b + 1)

            def norm(n, h_free):
                batch = {0: 0, 2: 3, 3: 5}.get(n)
                if batch is not None:
                    eng.wait_ge(ss_ready, 2 * n + 2)
                    rstd(ssq[:, 2 * n:2 * n + 2], D)
                    split(batch)
                eng.wait_ge(gam_in, 16 * (n + 1))
                for f in h_free:
                    eng.wait_ge(*f)
                for cc in range(4):
                    s, cs = cc // 2, slice(512 * (cc % 2), 512 * (cc % 2) + 512)
                    eng.wait_ge(sc_ready, 4 * n + cc + 1)
                    eng.scalar_tensor_tensor(h[:, s, cs], bank[6 + cc % 2][:, :], 1.0, gam[:, cs], ALU.add,
                                             ALU.mult).then_inc(sc_used, 1)
                if batch is None:
                    eng.wait_ge(ss_ready, 2 * n + 2)
                    rstd(ssq[:, 2 * n:2 * n + 2], D)
                eng.wait_ge(sc_used, 4 * n + 4)
                eng.sem_inc(gam_used, 1)
                for cc in range(4):
                    s, cs = cc // 2, slice(512 * (cc % 2), 512 * (cc % 2) + 512)
                    hs = h[:, s, cs]
                    chain(eng.scalar_tensor_tensor(hs, x[:, s, cs], ssq[:, 2 * n + s:2 * n + s + 1], hs, ALU.mult,
                                                   ALU.mult))
                    eng.wait_ge(sh_ready, 4 * n + cc + 1)
                    eng.tensor_tensor(hs, hs, bank[cc][:, :], ALU.add).then_inc(h_ready, 1)

            def residual(r):
                for ri in range(4 * r, 4 * r + 4):
                    s, hf = (ri % 4) // 2, ri % 2
                    cs = slice(512 * hf, 512 * hf + 512)
                    eng.wait_ge(res_ready, ri + 1)
                    eng.wait_ge(gate_sb, ri + 1)
                    ins = eng.tensor_tensor(tmp, bank[ri % 4][:, :], gate[:, ri % 2, :], ALU.mult)
                    ins.then_inc(res_used, 1)
                    eng.wait_ge(res_used, ri + 1)
                    if r == 2:
                        eng.wait_ge(ps_in, 16)
                        chain(eng.tensor_tensor(tmp, tmp, pscale[:, cs], ALU.mult))
                    ins = eng.tensor_tensor(x[:, s, cs], x[:, s, cs], tmp, ALU.add)
                    if hf:
                        ins.then_inc(x_ready, 1)
                        eng.wait_ge(x_ready, 2 * r + s + 1)
                    else:
                        chain(ins)

            def r2(a, n=16):
                return rt[:, a:a + 2 * n].rearrange("p (s e) -> p s e", s=NS)

            def bcast(ap, shape):
                return ap.broadcast_to(shape)

            def first_of(out, v, m, w, rank, n):
                shape = [P, NS, n]
                chain(eng.tensor_reduce(m, v, axis=AX_X, op=ALU.max))
                chain(eng.tensor_tensor(w, v, m.unsqueeze(2).broadcast_to(shape), ALU.is_equal))
                chain(eng.tensor_tensor(w, w, rank.unsqueeze(1).broadcast_to(shape), ALU.mult))
                chain(eng.tensor_reduce(m, w, axis=AX_X, op=ALU.max))
                chain(eng.tensor_tensor(out, w, m.unsqueeze(2).broadcast_to(shape), ALU.is_equal))

            def route(l):
                sc, sel, pair = r2(0), r2(32), rt[:, 64:112].rearrange("p (s g q) -> p s g q", s=NS, g=4)
                gs, w4, g1h = (rt[:, 112 + 8 * i:120 + 8 * i].rearrange("p (s g) -> p s g", s=NS) for i in range(3))
                w16, one1, one2, m = r2(160), r2(192), r2(224), rt[:, 256:258]
                ing, mask = r2(288), r2(320)
                eng.wait_ge(lgT_psum, l + 1)
                eng.tensor_copy(lgT[:, :], bank[7][:, 0:NS * P]).then_inc(lgT_sb, 1)
                eng.wait_ge(router_exp, l + 1)
                f = rt[:, 0:32]
                chain(eng.tensor_scalar(f, f, 1.0, None, ALU.add))
                chain(eng.reciprocal(f, f))
                chain(eng.tensor_tensor(sel, sc, rb[:, :].unsqueeze(1).broadcast_to([P, NS, NE]), ALU.add))
                v = rt[:, 32:64].rearrange("p (s g e) -> p s g e", s=NS, g=4)
                for s in range(NS):
                    vs, ps = v[:, s], pair[:, s]
                    eng.tensor_tensor(ps[:, :, 0:2], vs[:, :, 0:2], vs[:, :, 2:4], ALU.add)
                    eng.tensor_tensor(ps[:, :, 2:4], vs[:, :, 0:4:2], vs[:, :, 1:4:2], ALU.add)
                    eng.tensor_tensor(ps[:, :, 4:5], vs[:, :, 0:1], vs[:, :, 3:4], ALU.add)
                    chain(eng.tensor_tensor(ps[:, :, 5:6], vs[:, :, 1:2], vs[:, :, 2:3], ALU.add))
                chain(eng.tensor_reduce(gs, pair, axis=AX_X, op=ALU.max))
                first_of(g1h, gs, m, w4, col(C_RANK + 16, 4), 4)
                chain(eng.tensor_copy(ing.rearrange("p s (g e) -> p s g e", g=4),
                                      g1h.unsqueeze(3).broadcast_to([P, NS, 4, 4])))
                chain(eng.tensor_tensor(sel, sel, ing, ALU.mult))
                chain(eng.tensor_scalar(ing, ing, 1.0, BIG, ALU.subtract, ALU.mult))
                chain(eng.tensor_tensor(sel, sel, ing, ALU.add))
                first_of(one1, sel, m, w16, col(C_RANK, 16), 16)
                chain(eng.scalar_tensor_tensor(sel, one1, -4.0 * BIG, sel, ALU.mult, ALU.add))
                first_of(one2, sel, m, w16, col(C_RANK, 16), 16)
                eng.tensor_tensor(mask, one1, one2, ALU.add).then_inc(chosen, 1)
                eng.wait_ge(chosen, l + 1)
                chain(eng.tensor_tensor(w16, mask, sc, ALU.mult))
                chain(eng.tensor_reduce(m, w16, axis=AX_X, op=ALU.add))
                chain(eng.reciprocal(m, m))
                chain(eng.tensor_tensor(gt[:, :, 0:NE], w16, m.unsqueeze(2).broadcast_to([P, NS, NE]), ALU.mult))
                eng.wait_ge(pos_psum, l + 1)
                pp = bank[6][:, 64:96].rearrange("p (s e) -> p s e", s=NS)
                chain(eng.scalar_tensor_tensor(w16, pp, 1.0, mask, ALU.add, ALU.mult))
                chain(eng.tensor_scalar(posm[:, :, 0:NE], w16, 1.0, None, ALU.subtract))
                eng.tensor_reduce(cnt[:, :], bank[6][0:1, 96:112].rearrange("p (a b) -> p a b", b=2), axis=AX_X,
                                  op=ALU.max).then_inc(routed, 1)
                eng.wait_ge(routed, l + 1)

            def one_hot(dst, e, q):
                shape = [P, NS, 2, CAP]
                return eng.tensor_tensor(dst.rearrange("p s (e c) -> p s e c", e=2),
                                         posm[:, :, bass.ds(e, 2)].unsqueeze(3).broadcast_to(shape),
                                         col(C_IOTA + q * CAP, CAP).unsqueeze(1).unsqueeze(1).broadcast_to(shape),
                                         ALU.is_equal)

            def pair(l, p, it=None):
                ln = NPAIR * l
                t = 0 if it is None else 3 * it
                e = 2 * p if it is None else 6 * it + 2 * p
                n = eng.value_load(cnt[0:1, bass.ds(t + p, 1)], min_val=0, max_val=NS * P)

                def tile(q):
                    base = 18 * (ln + p) + 6 * q + (0 if it is None else 54 * it)
                    one_hot(o_S, e, q + 1)
                    one_hot(o_Sg, e, q + 1)
                    eng.drain()
                    v = o_Sg.rearrange("p s (e c) -> p s e c", e=2)
                    eng.tensor_tensor(v, v, gt[:, :, bass.ds(e, 2)].unsqueeze(3).broadcast_to([P, NS, 2, CAP]),
                                      ALU.mult).then_inc(ovf_dve, 1)
                    eng.wait_ge(ovf_pe, base + 1)
                    eng.tensor_copy(xs[:, 0:512], bank[6][:, :])
                    eng.tensor_copy(xs[:, 512:1024], bank[7][:, :]).then_inc(ovf_dve, 1)
                    eng.wait_ge(ovf_pe, base + 2)
                    eng.tensor_copy(hTf[:, 0:512], bank[4][:, :])
                    eng.tensor_copy(hTf[:, 512:1024], bank[5][:, :]).then_inc(ovf_dve, 1)
                    eng.wait_ge(ovf_act, 3 * (ln + p) + q + 1 + (0 if it is None else 9 * it))
                    eng.tensor_tensor(act, act, bank[5][:, :], ALU.mult).then_inc(ovf_dve, 1)
                    eng.wait_ge(ovf_pe, base + 4)
                    eng.tensor_copy(work[:, 2560:3072], bank[4][:, :])
                    eng.tensor_copy(work[:, 3072:3328], bank[5][:, 0:256]).then_inc(ovf_dve, 1)
                    eng.wait_ge(ovf_pe, base + 5)
                    eng.tensor_copy(ysb[:, 0, :], bank[6][:, :])
                    eng.tensor_copy(ysb[:, 1, :], bank[7][:, :]).then_inc(ovf_dve, 1)

                with eng.If(n > CAP):
                    tile(0)
                    with eng.If(n > 2 * CAP):
                        tile(1)
                        tile(2)
                    with eng.Else():
                        eng.wait_ge(ovf_dve, 18 * (ln + p) + 6 + (0 if it is None else 54 * it))
                        eng.sem_inc(ovf_dve, 12)
                    eng.nop()
                with eng.Else():
                    eng.sem_inc(ovf_dve, 18)

                eng.wait_ge(gat_done, 2 * t + 2 * (9 * l + p + 1))
                one_hot(S, e + 2, 0).then_inc(S_ready, 1)
                one_hot(Sg, e, 0).then_inc(Sg_half, 1)
                eng.wait_ge(Sg_half, t + (ln + p + 1))
                v = Sg.rearrange("p s (e c) -> p s e c", e=2)
                eng.tensor_tensor(v, v, gt[:, :, bass.ds(e, 2)].unsqueeze(3).broadcast_to([P, NS, 2, CAP]),
                                  ALU.mult).then_inc(Sg_ready, 1)
                eng.wait_ge(silu_done, t + (ln + p + 1))
                eng.wait_ge(up_done, t + (ln + p + 1))
                eng.tensor_tensor(act, act, bank[5][:, :], ALU.mult).then_inc(act_ready, 1)
                eng.wait_ge(actT_psum, 2 * t + (2 * (ln + p) + 1))
                eng.tensor_copy(work[:, 2560:3072], bank[4][:, :]).then_inc(actT_ready, 1)
                eng.wait_ge(actT_psum, 2 * t + (2 * (ln + p) + 2))
                eng.tensor_copy(work[:, 3072:3328], bank[5][:, 0:256]).then_inc(ST_ready, 1)
                eng.wait_ge(down_done, t + (ln + p + 1))
                eng.tensor_copy(ysb[:, 1, :], bank[7][:, :]).then_inc(y_dve, 1)
                eng.wait_ge(xgT_psum, t + (9 * l + p + 2))
                eng.tensor_copy(work[:, 1536:2048], bank[5][:, :]).then_inc(xg_dve, 1)

            def moe(l):
                route(l)
                one_hot(S, 0, 0).then_inc(S_ready, 1)
                eng.wait_ge(xgT_psum, 9 * l + 1)
                eng.tensor_copy(work[:, 1536:2048], bank[5][:, :]).then_inc(xg_dve, 1)
                pair(l, 0)
                pair(l, 1)
                with eng.Fori(0, 2) as it:
                    for p in range(2, 5):
                        pair(l, p, it)

            eng.memset(zero_b[:, :], 0.0)
            eng.memset(rwp[:, :, :], 0.0)
            eng.memset(posm[:, :, :], -1.0)
            eng.memset(gt[:, :, :], 0.0)
            eng.memset(condT[:, :, :], 0.0).then_inc(zeroed, 1)
            eng.wait_ge(tab_in, 16)
            eng.tensor_copy(sel_b[:, :], col(C_SEL, NS * P)).then_inc(sel_ready, 1)
            eng.wait_ge(cond_ready, NPART)
            norm(0, ())
            eng.wait_ge(attn_in, 16 * 13)
            eng.tensor_copy(rwp[:, :, 0:NE], rw[:, :, :]).then_inc(rw_ready, 1)
            chain(eng.tensor_tensor(lams[:, 0:128], lams[:, 0:128], lams[:, 128:256], ALU.mult))
            eng.tensor_reduce(lamv[:, 0:2], lams[:, 0:128].rearrange("p (a n) -> p a n", a=2), axis=AX_X,
                              op=ALU.add).then_inc(lam_dots, 1)
            eng.wait_ge(pre_psum, 1)
            eng.tensor_copy(kTs[:, :, 0:P], bank[4][:, :].rearrange("p (h t) -> p h t", h=H)).then_inc(pre_evac, 1)
            eng.wait_ge(pre_psum, 2)
            eng.tensor_copy(work[:, 512:1024], bank[5][:, :]).then_inc(pre_evac, 1)
            split(1)
            for i in range(4):
                t, s = i // 2, i % 2
                eng.wait_ge(win_evac, i + 1)
                v = qk[:, s, t, :]
                v8 = v.rearrange("p (m d) -> p m d", m=8)
                t8 = tmp.rearrange("p (m d) -> p m d", m=8)
                chain(eng.tensor_tensor(tmp, v, v, ALU.mult))
                chain(eng.tensor_reduce(qss, t8, axis=AX_X, op=ALU.add))
                rstd(qss, DH)
                chain(eng.tensor_tensor(v8, v8, qss.unsqueeze(2).broadcast_to([P, 8, DH]), ALU.mult))
                last = eng.tensor_tensor(v8, v8, (qg, kg)[t].unsqueeze(1).broadcast_to([P, 8, DH]), ALU.mult)
                if s == 1:
                    chain(last)
                    r8 = prob[1][:, 0, 0:2, :].rearrange("p a b -> p (a b)").rearrange("p (m d) -> p m d", m=8)
                    eng.tensor_tensor(t8, v8, col(C_COS, 64).unsqueeze(1).broadcast_to([P, 8, 64]), ALU.mult)
                    for half in range(2):
                        for pt in range(2):
                            o, f = 32 * half + 16 * pt, 32 * half + 16 * (1 - pt)
                            last = eng.tensor_tensor(r8[:, :, o:o + 16], v8[:, :, f:f + 16],
                                                     col(C_SIN + o, 16).unsqueeze(1).broadcast_to([P, 8, 16]), ALU.mult)
                    chain(last)
                    last = eng.tensor_tensor(v8, t8, r8, ALU.add)
                last.then_inc(qk_ready, 1)
                eng.wait_ge(qk_ready, i + 1)
            for g in range(4):
                eng.wait_ge(sg_psum, g // 2 + 1)
                mixed = bank[g // 2][:, 256 * (g % 2):256 * (g % 2) + 256].rearrange("p (s n) -> p s n", s=NS)
                eng.scalar_tensor_tensor(h[:, :, 512 + g * P:512 + (g + 1) * P], mixed, sgbT[:, g:g + 1],
                                         gu[:, :, g * P:(g + 1) * P], ALU.add, ALU.mult).then_inc(sg_used, 1)
            for i, dst in enumerate((qT[:, 0, :, :], kTp)):
                eng.wait_ge(qkT_psum, i + 1)
                eng.tensor_copy(dst, bank[2 + i][:, :].rearrange("p (h t) -> p h t", h=H)).then_inc(qkT_dve, 1)
            for g, (s, b0, heads) in enumerate(((0, 0, 4), (1, 2, 2), (1, 4, 2))):
                eng.wait_ge(score_psum, g + 1)
                h0 = 2 if g == 2 else 0
                for cm in range(2):
                    chain(eng.tensor_reduce(mx[:, s, cm, h0:h0 + heads],
                                            bank[b0 + cm][:, :].rearrange("p (h t) -> p h t", h=heads),
                                            axis=AX_X, op=ALU.max))
                m = mx[:, s, :, h0:h0 + heads]
                eng.tensor_scalar(m, m, -(DH ** -0.5), None, ALU.mult).then_inc(mx_ready, 1)
            eng.wait_ge(lam_exp, 1)
            chain(eng.tensor_tensor(lamv[:, 0:1], lamv[:, 2:3], lamv[:, 3:4], ALU.subtract))
            chain(eng.tensor_scalar(lamv[:, 0:1], lamv[:, 0:1], LAM0, None, ALU.add))
            for s in range(NS):
                eng.wait_ge(exp_ready, 1 + 2 * s)
                es = esum[:, s, :, :]
                chain(eng.reciprocal(es, es))
                chain(eng.tensor_scalar(esum[:, s, 1, :], esum[:, s, 1, :], lamv[:, 0:1], None, ALU.mult))
                for hh in range(H):
                    p0, p1 = prob[s][:, 0, hh, :], prob[s][:, 1, hh, :]
                    chain(eng.tensor_scalar(p1, p1, esum[:, s, 1, hh:hh + 1], None, ALU.mult))
                    eng.scalar_tensor_tensor(p0, p0, esum[:, s, 0, hh:hh + 1], p1, ALU.mult,
                                             ALU.subtract).then_inc(a_map, 1)
            eng.wait_ge(oss_ready, NS)
            rstd(oss, P)
            for s in range(NS):
                h4 = h[:, s, 0:512].rearrange("p (h n) -> p h n", h=H)
                chain(eng.tensor_tensor(h4, bank[3 + s][:, :].rearrange("p (h n) -> p h n", h=H),
                                        oss[:, H * s:H * (s + 1)].unsqueeze(2).broadcast_to([P, H, P]), ALU.mult))
                eng.scalar_tensor_tensor(h4, h4, 1.0 - LAM0, subg.unsqueeze(1).broadcast_to([P, H, P]),
                                         ALU.mult, ALU.mult).then_inc(att_ready, 1)
            split(2)
            residual(0)
            norm(1, ((tr_psum, 8),))
            moe(0)
            residual(1)
            norm(2, ((scat_done, NPAIR),))
            split(4)
            residual(2)
            norm(3, ((dT_psum, 4),))
            moe(1)
            residual(3)


_INS = ['x_prompt', 'x_sample', 'cache_k', 'cache_v', 'c', 'c_ctx', 'norm1_g', 'norm2_g', 'w_ada', 'b_ada',
        'w_in', 'w_out', 'q_norm_g', 'k_norm_g', 'lam_q1', 'lam_k1', 'lam_q2', 'lam_k2', 'subln_g',
        'sg_w', 'sg_b', 'pool_w', 'pool_scale', 'router_w', 'router_b', 'w_gate', 'w_up', 'w_down']
_OUTS = [(1, P, D), (1, P, D), (1, 1, P, H, 2, DH), (1, 1, P, H, 2 * DH)]


def kernel(**inputs):
    import numpy as _np
    import concourse.bacc as _bacc
    from concourse import mybir as _mybir
    from concourse.bass_utils import run_bass_kernel_spmd as _run

    nc = _bacc.Bacc("TRN2", target_bir_lowering=False, num_devices=1)
    arrays, args = {}, []
    for name in _INS:
        a = _np.asarray(inputs[name])
        a = _np.ascontiguousarray(a.transpose(0, 2, 1) if name == "sg_b" else a)
        arrays[f"in_{name}_dram"] = a
        args.append(nc.dram_tensor(f"in_{name}_dram", a.shape, _mybir.dt.from_np(a.dtype), kind="ExternalInput").ap())
    t = constant_table()
    arrays["in_table_dram"] = t
    args.append(nc.dram_tensor("in_table_dram", t.shape, _mybir.dt.float32, kind="ExternalInput").ap())
    for i, shape in enumerate(_OUTS):
        args.append(nc.dram_tensor(f"out_{i}_dram", shape, _mybir.dt.float32, kind="ExternalOutput").ap())
    trunk_kernel(nc, *args)
    r = _run(nc, [arrays], core_ids=[0])
    return tuple(r.results[0][f"out_{i}_dram"] for i in range(len(_OUTS)))
```

```python
from contextlib import ExitStack
import math

import numpy as np
import concourse.bass as bass
from concourse import mybir

F32 = mybir.dt.float32
I32 = mybir.dt.int32
BF16 = mybir.dt.bfloat16
ALU = mybir.AluOpType
ACT = mybir.ActivationFunctionType
AX_X = mybir.AxisListType.X

P = 128
D = 1024
KD = D // P
NS = 2
H, DH = 4, 64
NE = 16
FF = 512
KF = FF // P
CAP = 64
NTILE = NS * P // CAP
SLOT = 4096
NSLOT = 9
LAM0 = 0.8 - 0.6 * math.exp(0.0)
EPS = 1e-6
NPART = 3
BIG = 1.0e30
GRID_W = 64
WINDOWS = (2, 4, 8, 16)
SH1, SC1, G1, SH2, SC2, G2 = range(6)

C_ID, C_UP, C_ONE, C_POOL = 0, 128, 256, 384
C_SEL = C_POOL + 4 * P
C_CMP = C_SEL + 2 * P
C_IOTA = C_CMP + NE
C_RANK = C_IOTA + NTILE * CAP
C_COS = C_RANK + 20
C_SIN = C_COS + 64
C_PART = C_SIN + 64
C_N = C_PART + NPART - 1


def constant_table():
    t = np.zeros((P, C_N), np.float32)
    i = np.arange(P)
    t[:, C_ID:C_ID + P] = np.eye(P)
    t[:, C_UP:C_UP + P] = i[:, None] < i[None, :]
    t[:, C_ONE:C_ONE + P] = 1.0
    for g, w in enumerate(WINDOWS):
        lo = np.clip(i - w // 2, 0, P)
        hi = np.clip(i - w // 2 + w, 0, P)
        band = ((i[:, None] >= lo[None, :]) & (i[:, None] < hi[None, :])) / (hi - lo)[None, :].astype(np.float32)
        t[:, C_POOL + g * P:C_POOL + (g + 1) * P] = band - np.eye(P)
    for s in range(NS):
        t[:, C_SEL + s * P:C_SEL + (s + 1) * P] = ((i % 32 < 2 * NPART) & (i % 2 == s))[:, None]
    for part in range(1, NPART):
        t[:, C_PART + part - 1] = -(i % 32 >= 2 * part).astype(np.float32)
    t[:, C_CMP:C_CMP + NE] = (i % 32)[:, None] == np.arange(NE)[None, :]
    t[:, C_IOTA:C_IOTA + NTILE * CAP] = np.arange(NTILE * CAP)
    t[:, C_RANK:C_RANK + 16] = 16 - np.arange(16)
    t[:, C_RANK + 16:C_RANK + 20] = 4 - np.arange(4)
    inv = np.float32(10000.0) ** (-np.arange(16, dtype=np.float32) / 16)
    for half, pos in enumerate((i // GRID_W, i % GRID_W)):
        ang = pos.astype(np.float32)[:, None] * inv[None, :]
        for part, sign in ((0, -1.0), (1, 1.0)):
            c = half * 32 + part * 16
            t[:, C_COS + c:C_COS + c + 16] = np.cos(ang)
            t[:, C_SIN + c:C_SIN + c + 16] = sign * np.sin(ang)
    return t


NPAIR = NE // 2
PAIR_UNITS = 6


def ring_plan():
    filled, last = [0] * NSLOT, [None] * NSLOT
    first = [("ada", 0, 0), ("ada", 1, 1), ("ada", 2, 2), ("ada", 3, 3), ("win", 0, 7), ("win", 1, 8),
             ("win", 2, 0), ("win", 3, 1), ("win", 4, 2), ("ada", 4, 3), ("ada", 5, 7), ("ada", 6, 8),
             ("ada", 7, 0), ("wout", 0, 1), ("wout", 1, 2), ("ada", 8, 3), ("ada", 9, 7), ("ada", 10, 8),
             ("ada", 11, 0)]
    second = [("ada", 12 + i, (7 + i) % NSLOT) for i in range(8)] + [("pool", 0, 6)]
    second += [("ada", 20 + i, (7 + i) % NSLOT) for i in range(4)]
    units, layers = {}, []
    for plan, start in ((first, 4), (second, 2)):
        for kind, u, slot in plan:
            filled[slot] += 1
            units[kind, u] = (slot, filled[slot], last[slot])
            last[slot] = (kind, u)
        layers.append((start, list(filled), list(last)))
        last = [None] * NSLOT
        for n in range(NPAIR * PAIR_UNITS):
            filled[(start + n) % NSLOT] += 1
    return [x[:2] for x in first], [x[:2] for x in second], units, layers


def trunk_kernel(nc, x_prompt, x_sample, cache_k, cache_v, c, c_ctx, norm1_g, norm2_g, w_ada, b_ada,
                 w_in, w_out, q_norm_g, k_norm_g, lam_q1, lam_k1, lam_q2, lam_k2, subln_g,
                 sg_w, sg_b, pool_w, pool_scale, router_w, router_b, w_gate, w_up, w_down, table,
                 y_prompt, y_sample, state_k, state_v):
    first_units, second_units, UNIT, LAYER = ring_plan()

    with ExitStack() as ctx:
        def sb(name, shape, dt=F32):
            return ctx.enter_context(nc.sbuf_tensor(name, shape, dt))

        def sem(name):
            return ctx.enter_context(nc.semaphore(name))

        ring = sb("ring", [P, NSLOT * SLOT])
        x = sb("x", [P, NS, D])
        h = sb("h", [P, NS, D])
        hT = sb("hT", [P, KD, NS * P])
        modp = sb("modp", [P, 3, 512], BF16)
        sel_b = sb("sel_b", [P, NS * P], BF16)
        tab = sb("tab", [P, C_N])
        gam = sb("gam", [P, D])
        bada = sb("bada", [32, 512])
        condT = sb("condT", [P, KD, 32])
        cond = sb("cond", [P, NS, KD])
        rwp = sb("rwp", [P, KD, 32])
        zero_b = sb("zero_b", [P, 512], BF16)
        rb = sb("rb", [P, NE])
        work = sb("work", [P, 3840])
        st = sb("st", [P, 9 * 8])
        rt = sb("rt", [P, 11 * 32 + 48])
        posm = sb("posm", [P, NS, NE + 2])
        gt = sb("gt", [P, NS, NE + 2])
        cnt = sb("cnt", [1, NE + NPAIR], I32)
        vecs = sb("vecs", [P, 2 * 64 + P + 4 + 4])
        bank = [ctx.enter_context(nc.psum_tensor(f"bank{i}", [P, 512], F32)) for i in range(8)]

        def col(a, n):
            return tab[:, a:a + n]

        ident, upper, ones = col(C_ID, P), col(C_UP, P), col(C_ONE, P)

        def slot(i, n=SLOT):
            return ring[:, i * SLOT:i * SLOT + n]

        at = [4 * SLOT]

        def take(n):
            at[0] += n
            assert at[0] <= 7 * SLOT
            return ring[:, at[0] - n:at[0]]

        qk = take(2048).rearrange("p (s t n) -> p s t n", s=NS, t=2)
        vv = take(1024).rearrange("p (s n) -> p s n", s=NS)
        gu = take(1024).rearrange("p (s n) -> p s n", s=NS)
        gv = take(1024).rearrange("p (s n) -> p s n", s=NS)
        ck = take(512)
        cv = take(512)
        qT = take(1024).rearrange("p (s h t) -> p s h t", s=NS, h=H)
        kTp = take(512).rearrange("p (h t) -> p h t", h=H)
        kTs = take(1024).rearrange("p (h t) -> p h t", h=H)
        prob = [take(1024).rearrange("p (c h t) -> p c h t", c=2, h=H),
                take(2048).rearrange("p (c h t) -> p c h t", c=2, h=H)]
        sgw = work[:, 0:512].rearrange("p (g q) -> p g q", g=4)
        sgwT = work[:, 512:1024].rearrange("p (g q) -> p g q", g=4)
        aTp = work[:, 0:512].rearrange("p (h t) -> p h t", h=H)
        aTs = work[:, 1024:2048].rearrange("p (h r t) -> p h r t", h=H, r=2)
        tmp = work[:, 2048:2560]
        xs = work[:, 0:1024]
        xg = work[:, 1024:2048].rearrange("p (k s) -> p k s", k=KD)
        act = work[:, 2048:2560]
        actT = work[:, 2560:3072].rearrange("p (k s) -> p k s", k=KF)
        ysb = work[:, 2048:3072].rearrange("p (q n) -> p q n", q=2)
        STg = work[:, 3072:3328].rearrange("p (s t) -> p s t", s=NS)
        S = work[:, 3328:3584].rearrange("p (s c) -> p s c", s=NS)
        Sg = work[:, 3584:3840].rearrange("p (s c) -> p s c", s=NS)
        gate = work[:, 1024:2048].rearrange("p (q n) -> p q n", q=2)
        rest = work[:, 2048:2560]
        lgT = work[:, 3072:3328]
        rw = work[:, 3072:3200].rearrange("p (k e) -> p k e", k=KD)
        pscale = work[:, 0:1024]
        sq_junk = work[:, 2560:3584]
        hTf = hT[:, :, :].rearrange("p k t -> p (k t)")
        o_xg = hTf[:, 0:512].rearrange("p (k s) -> p k s", k=4)
        o_up = hTf[0:CAP, 512:1024]
        o_S = hTf[:, 1024:1280].rearrange("p (s c) -> p s c", s=NS)
        o_Sg = hTf[:, 1280:1536].rearrange("p (s c) -> p s c", s=NS)
        lams = work[:, 2560:2816]
        qg, kg, subg = vecs[:, 0:64], vecs[:, 64:128], vecs[:, 128:256]
        lamv, sgbT = vecs[:, 256:260], vecs[:, 260:264]
        ssq = st[:, 0:8]
        qss = st[:, 8:16]
        oss = st[:, 16:24]
        mx = st[:, 24:40].rearrange("p (s c h) -> p s c h", s=NS, c=2)
        esum = st[:, 40:56].rearrange("p (s c h) -> p s c h", s=NS, c=2)

        w_landed = [sem(f"w_landed{i}") for i in range(NSLOT)]
        first_in, attn_in, gam_in, ps_in = sem("first_in"), sem("attn_in"), sem("gam_in"), sem("ps_in")
        sel_ready, mod_first = sem("sel_ready"), sem("mod_first")
        zeroed, cond_ready, lam_dots, lam_exp = sem("zeroed"), sem("cond_ready"), sem("lam_dots"), sem("lam_exp")
        ada_done, pool_done = sem("ada_done"), sem("pool_done")
        mod_ready, tab_in, x_in = sem("mod_ready"), sem("tab_in"), sem("x_in")
        ss_ready, sc_ready, sc_used = sem("ss_ready"), sem("sc_ready"), sem("sc_used")
        sh_ready, h_ready, rw_ready = sem("sh_ready"), sem("h_ready"), sem("rw_ready")
        gam_used = sem("gam_used")
        tr_psum, tr_done = sem("tr_psum"), sem("tr_done")
        pre_psum, pre_evac = sem("pre_psum"), sem("pre_evac")
        win_psum, win_evac, qk_ready = sem("win_psum"), sem("win_evac"), sem("qk_ready")
        qkT_psum, qkT_dve, qkT_act = sem("qkT_psum"), sem("qkT_dve"), sem("qkT_act")
        sg_psum, sg_used = sem("sg_psum"), sem("sg_used")
        score_psum, mx_ready, exp_ready, a_map = sem("score_psum"), sem("mx_ready"), sem("exp_ready"), sem("a_map")
        aT_psum, aT_sb, o_psum, att_ready = sem("aT_psum"), sem("aT_sb"), sem("o_psum"), sem("att_ready")
        oss_ready = sem("oss_ready")
        res_ready, gate_sb, res_used, x_ready = sem("res_ready"), sem("gate_sb"), sem("res_used"), sem("x_ready")
        lgT_psum, lgT_sb = sem("lgT_psum"), sem("lgT_sb")
        logit_psum, router_exp, chosen, pos_psum, routed = (sem("logit_psum"), sem("router_exp"),
                                                            sem("chosen"), sem("pos_psum"), sem("routed"))
        dT_psum, dT_sb = sem("dT_psum"), sem("dT_sb")
        S_ready, Sg_half, Sg_ready, gat_done = sem("S_ready"), sem("Sg_half"), sem("Sg_ready"), sem("gat_done")
        xs_ready, xgT_psum, xg_act, xg_dve = sem("xs_ready"), sem("xgT_psum"), sem("xg_act"), sem("xg_dve")
        gate_done, up_done, silu_done, act_ready = sem("gate_done"), sem("up_done"), sem("silu_done"), sem("act_ready")
        actT_psum, actT_ready, ST_ready = sem("actT_psum"), sem("actT_ready"), sem("ST_ready")
        down_half = sem("down_half")
        down_done, y_act, y_dve, scat_done = sem("down_done"), sem("y_act"), sem("y_dve"), sem("scat_done")
        ovf_pe, ovf_act, ovf_dve = sem("ovf_pe"), sem("ovf_act"), sem("ovf_dve")
        dve_step = sem("dve_step")
        state_out, y_out = sem("state_out"), sem("y_out")

        block = ctx.enter_context(nc.Block())

        def expert_weights(w, l, e, n):
            flat = w.rearrange("l e (p k) f -> (l e) p (k f)", k=n)
            return flat[bass.ds(NE * l + e, 1), :, :].rearrange("a p n -> p (a n)")

        ada_v = w_ada.rearrange("l (p k) n -> l p k n", k=KD)
        win_v = w_in[0].rearrange("(p k) n -> p k n", k=KD)
        wout_v = w_out[0].rearrange("(p k) n -> p k n", k=KD)
        pool_v = pool_w[0].rearrange("g (j p) n -> p (g j) n", p=P)

        @block.sync
        def _(eng):
            def wait_used(name):
                kind, u = name
                if kind == "ada":
                    eng.wait_ge(ada_done, u // 4 + 1)
                elif kind == "win":
                    eng.wait_ge(win_psum, 2 * u + 2)
                elif kind == "wout":
                    eng.wait_ge(res_ready, u + 3)
                else:
                    eng.wait_ge(pool_done, 1)

            def unit(name):
                i, _, before = UNIT[name]
                kind, u = name
                if before:
                    wait_used(before)
                if kind == "pool":
                    dst = slot(i, 2048).rearrange("p (m n) -> p m n", m=8)
                    eng.dma_start(dst, pool_v).then_inc(w_landed[i], 16)
                    return
                src = {"ada": lambda: ada_v[u // 12, :, :, 512 * (u % 12):512 * (u % 12) + 512],
                       "win": lambda: win_v[:, :, 512 * u:512 * u + 512],
                       "wout": lambda: wout_v[:, :, 512 * u:512 * u + 512]}[kind]()
                eng.dma_start(slot(i).rearrange("p (k n) -> p k n", k=KD), src).then_inc(w_landed[i], 16)

            def wait_expert_unit(l, n, it):
                done = (gate_done, up_done, down_done)[n % PAIR_UNITS // 2]
                eng.wait_ge(done, 3 * it + (NPAIR * l + n // PAIR_UNITS + 1))

            def load_pair(l, p, it):
                start, _, last_unit = LAYER[l]
                for j in range(PAIR_UNITS):
                    n = PAIR_UNITS * p + j
                    i = (start + n) % NSLOT
                    if n >= NSLOT:
                        wait_expert_unit(l, n - NSLOT, it)
                    elif last_unit[i]:
                        wait_used(last_unit[i])
                    elif l == 0 and i == 4:
                        eng.wait_ge(att_ready, 2)
                        eng.wait_ge(o_psum, 2)
                        eng.wait_ge(state_out, 32)
                    w, k = ((w_gate, KD), (w_up, KD), (w_down, KF))[j // 2]
                    eng.dma_start(slot(i), expert_weights(w, l, 6 * it + (2 * p + j % 2), k)).then_inc(w_landed[i], 16)

            for dst, src in ((cond[:, 0, :], c_ctx.rearrange("(p k) -> p k", k=KD)),
                             (cond[:, 1, :], c[0].rearrange("(p k) -> p k", k=KD)),
                             (bada[0:24, :], b_ada.rearrange("l (u n) -> (l u) n", n=512)),
                             (bada[24:32, :], b_ada[0].rearrange("(u n) -> u n", n=512)[0:8, :])):
                eng.dma_start(dst, src).then_inc(first_in, 16)
            for name in first_units:
                unit(name)
                if name == ("ada", 3):
                    eng.dma_start(tab[:, :], table[:, :]).then_inc(tab_in, 16)
                    eng.dma_start(x[:, 0, :], x_prompt[0]).then_inc(x_in, 16)
                    eng.dma_start(x[:, 1, :], x_sample[0]).then_inc(x_in, 16)
                    eng.dma_start(gam[:, :], norm1_g[0:1, :].broadcast_to([P, D])).then_inc(gam_in, 16)
                if name == ("win", 0):
                    for dst, src in ((ck, cache_k[0, 0].rearrange("t h c d -> t (h c d)")),
                                     (cv, cache_v[0, 0].rearrange("t h d -> t (h d)")),
                                     (sgw, sg_w[0].rearrange("g p q -> p g q")),
                                     (qg, q_norm_g[0:1, :].broadcast_to([P, 64])),
                                     (kg, k_norm_g[0:1, :].broadcast_to([P, 64])),
                                     (lams[:, 0:64], lam_q1[0:1, :].broadcast_to([P, 64])),
                                     (lams[:, 64:128], lam_q2[0:1, :].broadcast_to([P, 64])),
                                     (lams[:, 128:192], lam_k1[0:1, :].broadcast_to([P, 64])),
                                     (lams[:, 192:256], lam_k2[0:1, :].broadcast_to([P, 64])),
                                     (subg, subln_g[0:1, :].broadcast_to([P, P])),
                                     (sgbT, sg_b[0]),
                                     (rb[:, :], router_b.rearrange("(a n) -> a n", a=1).broadcast_to([P, NE])),
                                     (rw[:, :, :], router_w.rearrange("(p k) e -> p k e", k=KD))):
                        eng.dma_start(dst, src).then_inc(attn_in, 16)
            for l in range(2):
                load_pair(l, 0, 0)
                load_pair(l, 1, 0)
                with eng.Fori(0, 2) as it:
                    for p in range(2, 5):
                        load_pair(l, p, it)
                if l == 0:
                    for n, name in enumerate(second_units):
                        if n < NSLOT:
                            wait_expert_unit(0, NPAIR * PAIR_UNITS - NSLOT + n, 0)
                        unit(name)
            for s, y in enumerate((y_prompt, y_sample)):
                eng.wait_ge(x_ready, 7 + s)
                eng.dma_start(y[0], x[:, s, :]).then_inc(y_out, 16)
            eng.wait_ge(y_out, 32)

        @block.gpsimd
        def _(eng):
            eng.wait_ge(qk_ready, 3)
            eng.dma_start(state_k[0, 0].rearrange("t h c d -> t (h c d)"), qk[:, 0, 1, :]).then_inc(state_out, 16)
            eng.wait_ge(win_evac, 5)
            eng.dma_start(state_v[0, 0].rearrange("t h d -> t (h d)"), vv[:, 0, :]).then_inc(state_out, 16)
            eng.wait_ge(state_out, 32)

        def overflow(eng, own, per_tile, l, p, it, tile):
            t = 0 if it is None else 3 * it
            e0 = 2 * p if it is None else 6 * it + 2 * p
            per_expert = 3 * per_tile
            base = 2 * per_expert * (NPAIR * l + p)

            def so_far(n):
                return base + n if it is None else 6 * per_expert * it + (base + n)

            n = eng.value_load(cnt[0:1, bass.ds(t + (NE + p), 1)], min_val=0, max_val=NS * P)
            with eng.If(n > CAP):
                for j in range(2):
                    if j:
                        eng.wait_ge(own, so_far(per_expert))
                        eng.nop()
                    ne = eng.value_load(cnt[0:1, bass.ds(e0 + j, 1)], min_val=0, max_val=NS * P)
                    with eng.If(ne > CAP):
                        tile(j, 0)
                        with eng.If(ne > 2 * CAP):
                            tile(j, 1)
                            tile(j, 2)
                        with eng.Else():
                            eng.wait_ge(own, so_far(per_expert * j + per_tile))
                            eng.sem_inc(own, 2 * per_tile)
                        eng.nop()
                    with eng.Else():
                        eng.sem_inc(own, per_expert)
                    eng.nop()
            with eng.Else():
                eng.sem_inc(own, 2 * per_expert)

        def mod_unit(j, hf):
            return 2 * j + hf

        @block.tensor
        def _(eng):
            mm = nc.tensor.matmul

            def ada_products(b, chunks=range(KD), groups=range(4)):
                if b >= 2:
                    eng.wait_ge(mod_ready, b - 1)
                ws = {}
                for g in groups:
                    i, fill, _ = UNIT["ada", 4 * b + g]
                    eng.wait_ge(w_landed[i], 16 * fill)
                    ws[g] = slot(i).rearrange("p (k n) -> p k n", k=KD)
                for k in chunks:
                    for g in groups:
                        mm(bank[6 + b % 2][32 * g:32 * g + 32, :], condT[:, k, :], ws[g][:, k, :],
                           start=k == 0, stop=False, skip_group_check=True)

            def ada_bias(b):
                for g in range(4):
                    a = 4 * b + g
                    last = mm(bank[6 + b % 2][32 * g:32 * g + 2 * NPART, :],
                              ident[0:32, a:a + 1].broadcast_to([32, 2 * NPART]), bada[:, :],
                              start=False, stop=True, skip_group_check=True)
                last.then_inc(ada_done, 1)

            def ada_batch(b):
                ada_products(b)
                ada_bias(b)

            def broadcast_mod(out, l, j, hf, s):
                u = mod_unit(j, hf)
                g = u % 4
                eng.wait_ge(mod_ready, 3 * l + u // 4 + 1)
                return mm(out, sel_b[32 * g:32 * g + 32, s * P:(s + 1) * P],
                          modp[32 * g:32 * g + 32, u // 4 % 3, :], start=True, stop=True)

            def norm_scales(n, s):
                for hf in range(2):
                    if s:
                        eng.wait_ge(sc_used, 4 * n + hf + 1)
                    broadcast_mod(bank[6 + hf][:, :], n // 2, 3 * (n % 2) + 1, hf, s).then_inc(sc_ready, 1)

            def norm_shifts(n, s):
                for hf in range(2):
                    broadcast_mod(bank[2 * s + hf][:, :], n // 2, 3 * (n % 2), hf, s).then_inc(sh_ready, 1)

            def norm_modulation(n):
                for s in range(NS):
                    norm_scales(n, s)
                    norm_shifts(n, s)

            def transpose_rows(cidx, streams=range(NS)):
                for ii in range(4 * cidx + 2 * streams[0], 4 * cidx + 2 * streams[-1] + 2):
                    s, j = (ii % 4) // 2, ii % 2
                    if cidx != 1:
                        eng.wait_ge(h_ready, (0, None, 4, 12)[cidx] + 2 * s + 2)
                    if ii >= 2:
                        eng.wait_ge(tr_done, ii - 1)
                    for kk in range(4):
                        last = nc.tensor.transpose(bank[4 + j][:, kk * P:(kk + 1) * P],
                                                   h[:, s, 4 * j + kk::KD], ident)
                    last.then_inc(tr_psum, 1)

            def residual_gates(r, l, j):
                for ri in range(4 * r, 4 * r + 4):
                    if ri % 4 >= 2:
                        eng.wait_ge(gate_sb, ri - 1)
                    broadcast_mod(bank[4 + ri % 2][:, :], l, j, ri % 2, (ri % 4) // 2).then_inc(res_ready, 1)

            def route(l):
                eng.wait_ge(mod_ready, 3 * (l + 1))
                eng.wait_ge(sc_used, 4 * (2 * l + 2))
                eng.wait_ge(tr_done, 12 + 4 * l)
                eng.wait_ge(rw_ready, 1)
                for k in range(KD):
                    g = k % 4
                    last = mm(bank[7][32 * g:32 * g + 32, 0:NS * P], rwp[:, k, :], hT[:, k, :],
                              start=k < 4, stop=k >= 4, skip_group_check=True)
                last.then_inc(lgT_psum, 1)
                eng.wait_ge(lgT_sb, l + 1)
                for s in range(NS):
                    last = mm(bank[6][:, s * NE:(s + 1) * NE], lgT[:, s * P:(s + 1) * P], col(C_CMP, NE),
                              start=True, stop=True)
                last.then_inc(logit_psum, 1)
                for b in range(4):
                    mm(bank[b][:, :], zero_b[:, 0:P], zero_b[:, :], start=True, stop=False, skip_group_check=True)
                eng.wait_ge(chosen, l + 1)
                m0, m1 = [rt[:, 320 + s * NE:320 + (s + 1) * NE] for s in range(NS)]
                mm(bank[6][:, 64:80], upper, m0, start=True, stop=True)
                mm(bank[6][:, 80:96], ones, m0, start=True, stop=False)
                mm(bank[6][:, 80:96], upper, m1, start=False, stop=True)
                mm(bank[6][:, 96:112], ones, m0, start=True, stop=False)
                mm(bank[6][:, 96:112], ones, m1, start=False, stop=True).then_inc(pos_psum, 1)

            def gather(src, q):
                for s in range(NS):
                    last = mm(bank[6 + q][:, :], src[:, s, :], h[:, s, 512 * q:512 * q + 512],
                              start=s == 0, stop=s == NS - 1)
                return last

            def gathered_transposes():
                for k in range(KD):
                    last = nc.tensor.transpose(bank[4 + k // 4][:, (k % 4) * P:(k % 4 + 1) * P], xs[:, k::KD], ident)
                return last

            def side_by_side(out, lhs, wa, wb, nk):
                for k in range(nk):
                    for q, w in enumerate((wa, wb)):
                        last = mm(out[CAP * q:CAP * (q + 1), :], lhs[:, k, CAP * q:CAP * (q + 1)], w(k),
                                  start=k == 0, stop=k == nk - 1, skip_group_check=True)
                return last

            def project(out, lhs, slots):
                v = [slot(i).rearrange("p (k f) -> p k f", k=KD) for i in slots]
                return side_by_side(out, lhs, lambda k: v[0][:, k, :], lambda k: v[1][:, k, :], KD)

            def down(slots, q):
                v = [slot(i).rearrange("p (k d) -> p k d", k=KF) for i in slots]
                cs = slice(512 * q, 512 * q + 512)
                return side_by_side(bank[6 + q], actT, lambda k: v[0][:, k, cs], lambda k: v[1][:, k, cs], KF)

            def activation_transposes():
                for k in range(KF):
                    last = nc.tensor.transpose(bank[4][:, k * P:(k + 1) * P], act[:, k::KF], ident)
                return last

            def scatter_transposes(sg):
                for s in range(NS):
                    last = nc.tensor.transpose(bank[5][:, s * P:(s + 1) * P], sg[:, s, :], ident)
                return last

            def scatter():
                for s in range(NS):
                    for q in range(2):
                        last = mm(bank[2 * s + q][:, :], STg[:, s, :], ysb[:, q, :], start=False, stop=False,
                                  skip_group_check=True)
                return last

            def pair(l, p, it=None):
                start, filled, _ = LAYER[l]
                ln = NPAIR * l
                t = 0 if it is None else 3 * it
                slots, landed = [], []
                for j in range(PAIR_UNITS):
                    n = PAIR_UNITS * p + j
                    i = (start + n) % NSLOT
                    slots.append(i)
                    fills = filled[i] + 1 + sum((start + m) % NSLOT == i for m in range(n))
                    landed.append(16 * fills if it is None else 32 * it + 16 * fills)

                def wait_unit(*js):
                    for j in js:
                        eng.wait_ge(w_landed[slots[j]], landed[j])

                def tile(j, q):
                    base = 36 * (ln + p) + 18 * j + 6 * q + (0 if it is None else 108 * it)
                    wg, wu = [slot(slots[i + j]).rearrange("p (k f) -> p k f", k=KD) for i in (0, 2)]
                    wd = slot(slots[4 + j]).rearrange("p (k d) -> p k d", k=KF)
                    wait_unit(j, 2 + j, 4 + j)
                    eng.wait_ge(ovf_dve, base + 1)
                    for q2 in range(2):
                        for s in range(NS):
                            last = mm(bank[6][CAP * q2:CAP * (q2 + 1), :], o_S[:, s, CAP * q2:CAP * (q2 + 1)],
                                      h[:, s, :].rearrange("p (m k) -> p k m", k=KD)[:, 4 * q2:4 * q2 + 4, :],
                                      start=s == 0, stop=s == NS - 1, skip_group_check=True)
                    last.then_inc(ovf_pe, 1)
                    eng.wait_ge(ovf_dve, base + 2)
                    for k in range(4):
                        last = nc.tensor.transpose(bank[4][:, k * P:(k + 1) * P], xs[:, k * P:(k + 1) * P], ident)
                    last.then_inc(ovf_pe, 1)
                    eng.wait_ge(ovf_dve, base + 3)
                    for k in range(KD):
                        lhs = o_xg[:, k % 4, CAP * (k // 4):CAP * (k // 4 + 1)]
                        for q2, w in enumerate((wg, wu)):
                            last = mm(bank[4][CAP * q2:CAP * (q2 + 1), :], lhs, w[:, k, :],
                                      start=k == 0, stop=k == KD - 1, skip_group_check=True)
                    last.then_inc(ovf_pe, 1)
                    eng.wait_ge(ovf_dve, base + 4)
                    activation_transposes()
                    scatter_transposes(o_Sg).then_inc(ovf_pe, 1)
                    eng.wait_ge(ovf_dve, base + 5)
                    for k in range(KF):
                        for q2 in range(2):
                            last = mm(bank[6][CAP * q2:CAP * (q2 + 1), :], actT[:, k, 0:CAP],
                                      wd[:, k, 512 * q2:512 * q2 + 512],
                                      start=k == 0, stop=k == KF - 1, skip_group_check=True)
                    last.then_inc(ovf_pe, 1)
                    eng.wait_ge(ovf_dve, base + 6)
                    for q2 in range(2):
                        rows = slice(CAP * q2, CAP * (q2 + 1))
                        for s in range(NS):
                            last = mm(bank[2 * s + q2][:, :], STg[rows, s, :], ysb[rows, 0, :],
                                      start=False, stop=False, skip_group_check=True)
                    last.then_inc(ovf_pe, 1)

                eng.wait_ge(xg_act, t + (9 * l + p + 1))
                eng.wait_ge(xg_dve, t + (9 * l + p + 1))
                eng.nop()
                overflow(eng, ovf_pe, 6, l, p, it, tile)

                wait_unit(0, 1)
                project(bank[4], xg, slots[0:2]).then_inc(gate_done, 1)
                wait_unit(2, 3)
                project(bank[5], xg, slots[2:4]).then_inc(up_done, 1)
                eng.wait_ge(S_ready, t + (9 * l + p + 2))
                gather(S, 0).then_inc(gat_done, 1)
                eng.wait_ge(Sg_ready, t + (ln + p + 1))
                eng.wait_ge(act_ready, t + (ln + p + 1))
                activation_transposes().then_inc(actT_psum, 1)
                scatter_transposes(Sg).then_inc(actT_psum, 1)
                gather(S, 1).then_inc(gat_done, 1)
                wait_unit(4, 5)
                eng.wait_ge(actT_ready, t + (ln + p + 1))
                eng.wait_ge(xs_ready, 2 * t + (2 * (9 * l + p + 2) - 1))
                down(slots[4:6], 0).then_inc(down_half, 1)
                eng.wait_ge(xs_ready, 2 * t + 2 * (9 * l + p + 2))
                down(slots[4:6], 1).then_inc(down_done, 1)
                eng.wait_ge(ST_ready, t + (ln + p + 1))
                gathered_transposes().then_inc(xgT_psum, 1)
                eng.wait_ge(y_act, t + (ln + p + 1))
                eng.wait_ge(y_dve, t + (ln + p + 1))
                scatter().then_inc(scat_done, 1)

            def moe(l):
                eng.wait_ge(routed, l + 1)
                eng.wait_ge(S_ready, 9 * l + 1)
                gather(S, 0).then_inc(gat_done, 1)
                gather(S, 1).then_inc(gat_done, 1)
                eng.wait_ge(xs_ready, 2 * (9 * l + 1))
                gathered_transposes().then_inc(xgT_psum, 1)
                pair(l, 0)
                pair(l, 1)
                with eng.Fori(0, 2) as it:
                    for p in range(2, 5):
                        pair(l, p, it)
                eng.wait_ge(xg_act, 9 * (l + 1))
                eng.wait_ge(xg_dve, 9 * (l + 1))

            eng.wait_ge(cond_ready, NPART)
            ada_products(0, groups=(0, 1))
            ada_products(0, groups=(2, 3))
            eng.wait_ge(tab_in, 16)
            ada_bias(0)
            eng.wait_ge(sel_ready, 1)
            norm_modulation(0)
            transpose_rows(0, (0,))
            for i in range(10):
                u, s = i // 2, i % 2
                sl, fill, _ = UNIT[("win", u)]
                eng.wait_ge(w_landed[sl], 16 * fill)
                eng.wait_ge(tr_done, 2 * s + 2)
                if i >= 2:
                    eng.wait_ge(win_evac, i - 1)
                w = slot(sl).rearrange("p (k n) -> p k n", k=KD)
                for k in range(KD):
                    last = mm(bank[i % 2][:, :], hT[:, k, s * P:(s + 1) * P], w[:, k, :],
                              start=k == 0, stop=k == KD - 1)
                last.then_inc(win_psum, 1)
                if i == 0:
                    transpose_rows(0, (1,))
                    eng.wait_ge(attn_in, 16 * 13)
                    for b, src in ((2, ck.rearrange("p (h t) -> p h t", h=H)), (3, sgw)):
                        for k in range(4):
                            last = nc.tensor.transpose(bank[b][:, k * P:(k + 1) * P], src[:, k, :], ident)
                        last.then_inc(pre_psum, 1)
            eng.wait_ge(win_evac, 10)
            eng.wait_ge(pre_evac, 2)
            for g in range(4):
                last = mm(bank[g // 2][:, 256 * (g % 2):256 * (g % 2) + 256].rearrange("p (s n) -> p s n", s=NS),
                          sgwT[:, g, :], gv[:, :, g * P:(g + 1) * P], start=True, stop=True)
                if g % 2:
                    last.then_inc(sg_psum, 1)
            for i in range(4):
                s, t = i // 2, i % 2
                eng.wait_ge(qk_ready, (1, 3, 2, 4)[i])
                for hh in range(H):
                    last = nc.tensor.transpose(bank[2 + i][:, hh * P:(hh + 1) * P],
                                               qk[:, s, t, hh * P:(hh + 1) * P], ident)
                last.then_inc(qkT_psum, 1)

            def score(b, s, cmap, heads):
                keys, n = (kTp, P) if s == 0 else (kTs, 2 * P)
                r = slice(64 * cmap, 64 * cmap + 64)
                for q, hh in enumerate(heads):
                    last = mm(bank[b][:, q * n:(q + 1) * n], qT[r, s, hh, :], keys[r, hh, :], start=True, stop=True)
                return last

            eng.wait_ge(sg_used, 4)
            eng.wait_ge(qkT_dve, 2)
            score(0, 0, 0, range(4))
            score(1, 0, 1, range(4)).then_inc(score_psum, 1)
            eng.wait_ge(qkT_act, 2)
            for hp in range(2):
                score(2 + 2 * hp, 1, 0, (2 * hp, 2 * hp + 1))
                score(3 + 2 * hp, 1, 1, (2 * hp, 2 * hp + 1)).then_inc(score_psum, 1)
            ada_products(1, range(4))
            eng.wait_ge(a_map, 4)
            for hh in range(H):
                last = nc.tensor.transpose(bank[0][:, hh * P:(hh + 1) * P], prob[0][:, 0, hh, :], ident)
            last.then_inc(aT_psum, 1)
            for hp in range(2):
                eng.wait_ge(a_map, 6 + 2 * hp)
                for q in range(4):
                    last = nc.tensor.transpose(bank[1 + hp][:, q * P:(q + 1) * P],
                                               prob[1][:, 0, 2 * hp + q // 2, (q % 2) * P:(q % 2 + 1) * P], ident)
                last.then_inc(aT_psum, 1)
            eng.wait_ge(aT_sb, 1)
            for hh in range(H):
                last = mm(bank[3][:, hh * P:(hh + 1) * P], aTp[:, hh, :], vv[:, 0, hh * P:(hh + 1) * P],
                          start=True, stop=True)
            last.then_inc(o_psum, 1)
            eng.wait_ge(aT_sb, 3)
            for hh in range(H):
                o = bank[4][:, hh * P:(hh + 1) * P]
                mm(o, aTs[:, hh, 0, :], cv[:, hh * P:(hh + 1) * P], start=True, stop=False)
                last = mm(o, aTs[:, hh, 1, :], vv[:, 1, hh * P:(hh + 1) * P], start=False, stop=True)
            last.then_inc(o_psum, 1)
            ada_products(1, range(4, KD))
            ada_bias(1)
            eng.wait_ge(att_ready, 2)
            transpose_rows(1)
            for ri in range(4):
                s, u = ri // 2, ri % 2
                sl, fill, _ = UNIT[("wout", u)]
                eng.wait_ge(w_landed[sl], 16 * fill)
                eng.wait_ge(tr_done, 6 + 2 * s)
                w = slot(sl).rearrange("p (k n) -> p k n", k=KD)
                for k in range(KD):
                    last = mm(bank[ri][:, :], hT[:, k, s * P:(s + 1) * P], w[:, k, :],
                              start=k == 0, stop=k == KD - 1)
                    if ri == 3 and k == 3:
                        norm_scales(1, 0)
                        eng.wait_ge(res_used, 2)
                        norm_shifts(1, 0)
                eng.wait_ge(tr_done, 8)
                if ri >= 2:
                    eng.wait_ge(gate_sb, ri - 1)
                broadcast_mod(bank[4 + ri % 2][:, :], 0, G1, u, s).then_inc(res_ready, 1)
                if ri == 2:
                    ada_batch(2)
            norm_scales(1, 1)
            eng.wait_ge(res_used, 4)
            norm_shifts(1, 1)
            transpose_rows(2)
            route(0)
            moe(0)
            residual_gates(1, 0, G2)

            ada_batch(3)
            eng.wait_ge(res_used, 8)
            norm_modulation(2)
            sl, fill, _ = UNIT["pool", 0]
            pw = slot(sl, 2048).rearrange("p (g j n) -> p g j n", g=4, j=2)
            for s in range(NS):
                eng.wait_ge(h_ready, 8 + 2 * s + 2)
                for j in range(2):
                    for kk in range(4):
                        ch = 4 * j + kk
                        last = mm(bank[4 + j][:, kk * P:(kk + 1) * P], h[:, s, ch * P:(ch + 1) * P],
                                  col(C_POOL + (ch // 2) * P, P), start=True, stop=True)
                    last.then_inc(dT_psum, 1)
                if s == 0:
                    eng.wait_ge(dT_sb, 2)
            ada_batch(4)
            eng.wait_ge(w_landed[sl], 16 * fill)
            for s in range(NS):
                eng.wait_ge(dT_sb, 2 * s + 2)
                for g in range(4):
                    for j in range(2):
                        last = mm(bank[2 * s + g // 2][:, 256 * (g % 2):256 * (g % 2) + 256],
                                  hT[:, 2 * g + j, s * P:(s + 1) * P], pw[:, g, j, :], start=j == 0, stop=j == 1)
            last.then_inc(pool_done, 1)
            residual_gates(2, 1, G1)
            ada_batch(5)
            eng.wait_ge(res_used, 12)
            norm_modulation(3)
            transpose_rows(3)
            route(1)
            moe(1)
            residual_gates(3, 1, G2)

        @block.scalar
        def _(eng):
            def evac(dst, b, cols=slice(0, 512)):
                return eng.activation(dst, b[:, cols], ACT.Copy)

            def evac_mod(b):
                eng.wait_ge(ada_done, b + 1)
                evac(modp[:, b % 3, :], bank[6 + b % 2]).then_inc(mod_first, 1)

            def squares(n, s):
                if n:
                    eng.wait_ge(x_ready, 2 * (n - 1) + s + 1)
                if n == 1 and s:
                    eng.wait_ge(ss_ready, 3)
                eng.activation(sq_junk if n == 1 else hTf[:, s * D:(s + 1) * D], x[:, s, :], ACT.Square,
                               accum_out=ssq[:, 2 * n + s:2 * n + s + 1]).then_inc(ss_ready, 1)

            def evac_gate(ri):
                eng.wait_ge(res_ready, ri + 1)
                if ri % 4 >= 2:
                    eng.wait_ge(res_used, ri - 1)
                evac(gate[:, ri % 2, :], bank[4 + ri % 2]).then_inc(gate_sb, 1)

            def evac_gates(r):
                for ri in range(4 * r, 4 * r + 4):
                    evac_gate(ri)

            def evac_transposes(cidx):
                for ii in range(4 * cidx, 4 * cidx + 4):
                    s, j = (ii % 4) // 2, ii % 2
                    eng.wait_ge(tr_psum, ii + 1)
                    eng.activation(hT[:, 4 * j:4 * j + 4, s * P:(s + 1) * P],
                                   bank[4 + j][:, :].rearrange("p (k t) -> p k t", k=4),
                                   ACT.Copy).then_inc(tr_done, 1)

            def pair(l, p, it=None):
                ln = NPAIR * l
                t = 0 if it is None else 3 * it

                def tile(j, q):
                    eng.wait_ge(ovf_pe, 36 * (ln + p) + 18 * j + 6 * q + 3 + (0 if it is None else 108 * it))
                    eng.activation(act, bank[4][:, :], ACT.Silu)
                    eng.activation(o_up, bank[4][CAP:2 * CAP, :], ACT.Copy).then_inc(ovf_act, 1)

                overflow(eng, ovf_act, 1, l, p, it, tile)

                eng.wait_ge(gate_done, t + (ln + p + 1))
                eng.activation(act, bank[4][:, :], ACT.Silu).then_inc(silu_done, 1)
                for q in range(2):
                    eng.wait_ge(gat_done, 2 * t + (2 * (9 * l + p + 1) + q + 1))
                    evac(xs[:, 512 * q:512 * q + 512], bank[6 + q]).then_inc(xs_ready, 1)
                eng.wait_ge(down_half, t + (ln + p + 1))
                evac(ysb[:, 0, :], bank[6]).then_inc(y_act, 1)
                eng.wait_ge(xgT_psum, t + (9 * l + p + 2))
                evac(work[:, 1024:1536], bank[4]).then_inc(xg_act, 1)

            def moe(l):
                eng.wait_ge(logit_psum, l + 1)
                eng.activation(rt[:, 0:32], bank[6][:, 0:32], ACT.Exp, scale=-1.0).then_inc(router_exp, 1)
                for q in range(2):
                    eng.wait_ge(gat_done, 2 * 9 * l + q + 1)
                    evac(xs[:, 512 * q:512 * q + 512], bank[6 + q]).then_inc(xs_ready, 1)
                eng.wait_ge(xgT_psum, 9 * l + 1)
                evac(work[:, 1024:1536], bank[4]).then_inc(xg_act, 1)
                eng.wait_ge(routed, l + 1)
                pair(l, 0)
                pair(l, 1)
                with eng.Fori(0, 2) as it:
                    for p in range(2, 5):
                        pair(l, p, it)

            def load_gamma(v, used):
                eng.wait_ge(gam_used, used)
                eng.dma_start(gam[:, :], v.broadcast_to([P, D])).then_inc(gam_in, 16)

            eng.wait_ge(first_in, 16 * 4)
            eng.wait_ge(zeroed, 1)
            for i in range(NPART):
                eng.activation(condT[:, :, NS * i:NS * (i + 1)].rearrange("p k s -> p s k"), cond[:, :, :],
                               ACT.Silu).then_inc(cond_ready, 1)
            evac_mod(0)
            eng.wait_ge(x_in, 32)
            squares(0, 0)
            squares(0, 1)
            evac_transposes(0)
            for i in range(10):
                u, s = i // 2, i % 2
                eng.wait_ge(win_psum, i + 1)
                dst = (qk[:, s, 0, :], qk[:, s, 1, :], vv[:, s, :], gu[:, s, :], gv[:, s, :])[u]
                eng.activation(dst, bank[i % 2][:, :], ACT.Copy if u < 3 else ACT.Gelu_apprx_tanh).then_inc(win_evac, 1)
            load_gamma(norm2_g[0:1, :], 1)
            for i in (2, 3):
                eng.wait_ge(qkT_psum, i + 1)
                dst = qT[:, 1, :, :] if i == 2 else kTs[:, :, P:2 * P]
                eng.activation(dst, bank[2 + i][:, :].rearrange("p (h t) -> p h t", h=H), ACT.Copy).then_inc(qkT_act, 1)
            eng.wait_ge(lam_dots, 1)
            eng.activation(lamv[:, 2:4], lamv[:, 0:2], ACT.Exp).then_inc(lam_exp, 1)
            for g, (s, b0, heads) in enumerate(((0, 0, range(4)), (1, 2, (0, 1)), (1, 4, (2, 3)))):
                n = P if s == 0 else 2 * P
                eng.wait_ge(mx_ready, g + 1)
                for cm in range(2):
                    for q, hh in enumerate(heads):
                        last = eng.activation(prob[s][:, cm, hh, :], bank[b0 + cm][:, q * n:(q + 1) * n], ACT.Exp,
                                              bias=mx[:, s, cm, hh:hh + 1], scale=DH ** -0.5,
                                              accum_out=esum[:, s, cm, hh:hh + 1])
                last.then_inc(exp_ready, 1)
            for i, dst in enumerate((work[:, 0:512], work[:, 1024:1536], work[:, 1536:2048])):
                eng.wait_ge(aT_psum, i + 1)
                evac(dst, bank[i]).then_inc(aT_sb, 1)
            for s in range(NS):
                eng.wait_ge(o_psum, s + 1)
                for hh in range(H):
                    last = eng.activation(sq_junk[:, (H * s + hh) * P:(H * s + hh + 1) * P],
                                          bank[3 + s][:, hh * P:(hh + 1) * P], ACT.Square,
                                          accum_out=oss[:, H * s + hh:H * s + hh + 1])
                last.then_inc(oss_ready, 1)
            evac_mod(1)
            evac_transposes(1)
            evac_gate(0)
            evac_gate(1)
            squares(1, 0)
            evac_gate(2)
            evac_mod(2)
            evac_gate(3)
            squares(1, 1)
            evac_transposes(2)
            load_gamma(norm1_g[1:2, :], 2)
            moe(0)
            eng.wait_ge(scat_done, NPAIR)
            eng.dma_start(pscale, pool_scale[0:1, :].broadcast_to([P, D])).then_inc(ps_in, 16)
            eng.wait_ge(xg_dve, 9)
            evac_gates(1)
            squares(2, 0)
            squares(2, 1)
            evac_mod(3)
            for ii in range(4):
                s, j = ii // 2, ii % 2
                eng.wait_ge(dT_psum, ii + 1)
                eng.activation(hT[:, 4 * j:4 * j + 4, s * P:(s + 1) * P],
                               bank[4 + j][:, :].rearrange("p (k t) -> p k t", k=4), ACT.Copy).then_inc(dT_sb, 1)
            load_gamma(norm2_g[1:2, :], 3)
            evac_mod(4)
            evac_gates(2)
            squares(3, 0)
            squares(3, 1)
            evac_mod(5)
            evac_transposes(3)
            moe(1)
            eng.wait_ge(xg_dve, 18)
            evac_gates(3)

        @block.vector
        def _(eng):
            steps = [0]

            def chain(ins):
                steps[0] += 1
                ins.then_inc(dve_step, 1)
                eng.wait_ge(dve_step, steps[0])

            def rstd(v, n):
                w = v.shape[1]
                y, t = st[:, 56:56 + w], st[:, 64:64 + w]
                chain(eng.tensor_scalar(v, v, 1.0 / n, EPS, ALU.mult, ALU.add))
                chain(eng.tensor_scalar(t.bitcast(I32), v.bitcast(I32), 1, None, ALU.logical_shift_right))
                chain(eng.tensor_scalar(y.bitcast(I32), t.bitcast(I32), -1.0, float(0x5f3759df), ALU.mult, ALU.add))
                for i in range(3):
                    chain(eng.tensor_tensor(t, y, y, ALU.mult))
                    chain(eng.scalar_tensor_tensor(t, t, -0.5, v, ALU.mult, ALU.mult))
                    chain(eng.scalar_tensor_tensor(v if i == 2 else y, t, 1.5, y, ALU.add, ALU.mult))

            def split(b):
                eng.wait_ge(mod_first, b + 1)
                v, part = bank[6 + b % 2][:, :], modp[:, b % 3, :]
                chain(eng.scalar_tensor_tensor(rest, part, col(C_PART, 1), v, ALU.mult, ALU.add))
                chain(eng.tensor_copy(part, rest))
                eng.scalar_tensor_tensor(part, part, col(C_PART + 1, 1), rest, ALU.mult,
                                         ALU.add).then_inc(mod_ready, 1)
                eng.wait_ge(mod_ready, b + 1)

            def norm(n, s):
                streams = 1 if n == 1 else NS
                if s == 0:
                    if n:
                        eng.wait_ge(ss_ready, 2 * n + streams)
                        rstd(ssq[:, 2 * n:2 * n + streams], D)
                    split((0, 2, 3, 5)[n])
                eng.wait_ge(gam_in, 16 * (n + 1))
                for hf in range(2):
                    cs = slice(512 * hf, 512 * hf + 512)
                    eng.wait_ge(sc_ready, 4 * n + 2 * s + hf + 1)
                    eng.scalar_tensor_tensor(h[:, s, cs], bank[6 + hf][:, :], 1.0, gam[:, cs], ALU.add,
                                             ALU.mult).then_inc(sc_used, 1)
                if (n, s) == (0, 0):
                    eng.wait_ge(ss_ready, 2)
                    rstd(ssq[:, 0:2], D)
                elif (n, s) == (1, 1):
                    eng.wait_ge(ss_ready, 4)
                    rstd(ssq[:, 3:4], D)
                eng.wait_ge(sc_used, 4 * n + 2 * s + 2)
                if s:
                    eng.sem_inc(gam_used, 1)
                for hf in range(2):
                    cs = slice(512 * hf, 512 * hf + 512)
                    hs = h[:, s, cs]
                    chain(eng.scalar_tensor_tensor(hs, x[:, s, cs], ssq[:, 2 * n + s:2 * n + s + 1], hs, ALU.mult,
                                                   ALU.mult))
                    eng.wait_ge(sh_ready, 4 * n + 2 * s + hf + 1)
                    eng.tensor_tensor(hs, hs, bank[2 * s + hf][:, :], ALU.add).then_inc(h_ready, 1)

            def residual(r, s):
                for hf in range(2):
                    ri = 4 * r + 2 * s + hf
                    cs = slice(512 * hf, 512 * hf + 512)
                    eng.wait_ge(res_ready, ri + 1)
                    eng.wait_ge(gate_sb, ri + 1)
                    ins = eng.tensor_tensor(tmp, bank[ri % 4][:, :], gate[:, ri % 2, :], ALU.mult)
                    ins.then_inc(res_used, 1)
                    eng.wait_ge(res_used, ri + 1)
                    if r == 2:
                        eng.wait_ge(ps_in, 16)
                        chain(eng.tensor_tensor(tmp, tmp, pscale[:, cs], ALU.mult))
                    ins = eng.tensor_tensor(x[:, s, cs], x[:, s, cs], tmp, ALU.add)
                    if hf:
                        ins.then_inc(x_ready, 1)
                        eng.wait_ge(x_ready, 2 * r + s + 1)
                    else:
                        chain(ins)

            def r2(a, n=16):
                return rt[:, a:a + 2 * n].rearrange("p (s e) -> p s e", s=NS)

            def first_of(out, v, m, w, rank, n):
                shape = [P, NS, n]
                chain(eng.tensor_reduce(m, v, axis=AX_X, op=ALU.max))
                chain(eng.tensor_tensor(w, v, m.unsqueeze(2).broadcast_to(shape), ALU.is_equal))
                chain(eng.tensor_tensor(w, w, rank.unsqueeze(1).broadcast_to(shape), ALU.mult))
                chain(eng.tensor_reduce(m, w, axis=AX_X, op=ALU.max))
                chain(eng.tensor_tensor(out, w, m.unsqueeze(2).broadcast_to(shape), ALU.is_equal))

            def route(l):
                sc, sel, pair = r2(0), r2(32), rt[:, 64:112].rearrange("p (s g q) -> p s g q", s=NS, g=4)
                gs, w4, g1h = (rt[:, 112 + 8 * i:120 + 8 * i].rearrange("p (s g) -> p s g", s=NS) for i in range(3))
                w16, one1, one2, m = r2(160), r2(192), r2(224), rt[:, 256:258]
                ing, mask = r2(288), r2(320)
                eng.wait_ge(lgT_psum, l + 1)
                eng.tensor_copy(lgT[:, :], bank[7][:, 0:NS * P]).then_inc(lgT_sb, 1)
                eng.wait_ge(router_exp, l + 1)
                f = rt[:, 0:32]
                chain(eng.tensor_scalar(f, f, 1.0, None, ALU.add))
                chain(eng.reciprocal(f, f))
                chain(eng.tensor_tensor(sel, sc, rb[:, :].unsqueeze(1).broadcast_to([P, NS, NE]), ALU.add))
                v = rt[:, 32:64].rearrange("p (s g e) -> p s g e", s=NS, g=4)
                for s in range(NS):
                    vs, ps = v[:, s], pair[:, s]
                    eng.tensor_tensor(ps[:, :, 0:2], vs[:, :, 0:2], vs[:, :, 2:4], ALU.add)
                    eng.tensor_tensor(ps[:, :, 2:4], vs[:, :, 0:4:2], vs[:, :, 1:4:2], ALU.add)
                    eng.tensor_tensor(ps[:, :, 4:5], vs[:, :, 0:1], vs[:, :, 3:4], ALU.add)
                    chain(eng.tensor_tensor(ps[:, :, 5:6], vs[:, :, 1:2], vs[:, :, 2:3], ALU.add))
                chain(eng.tensor_reduce(gs, pair, axis=AX_X, op=ALU.max))
                first_of(g1h, gs, m, w4, col(C_RANK + 16, 4), 4)
                chain(eng.tensor_scalar(ing.rearrange("p s (g e) -> p s g e", g=4),
                                        g1h.unsqueeze(3).broadcast_to([P, NS, 4, 4]), 1.0, BIG,
                                        ALU.subtract, ALU.mult))
                chain(eng.tensor_tensor(sel, sel, ing, ALU.add))
                first_of(one1, sel, m, w16, col(C_RANK, 16), 16)
                chain(eng.scalar_tensor_tensor(sel, one1, -4.0 * BIG, sel, ALU.mult, ALU.add))
                first_of(one2, sel, m, w16, col(C_RANK, 16), 16)
                eng.tensor_tensor(mask, one1, one2, ALU.add).then_inc(chosen, 1)
                eng.wait_ge(chosen, l + 1)
                chain(eng.tensor_tensor(w16, mask, sc, ALU.mult))
                chain(eng.tensor_reduce(m, w16, axis=AX_X, op=ALU.add))
                chain(eng.reciprocal(m, m))
                chain(eng.tensor_tensor(gt[:, :, 0:NE], w16, m.unsqueeze(2).broadcast_to([P, NS, NE]), ALU.mult))
                eng.wait_ge(pos_psum, l + 1)
                pp = bank[6][:, 64:96].rearrange("p (s e) -> p s e", s=NS)
                chain(eng.scalar_tensor_tensor(w16, pp, 1.0, mask, ALU.add, ALU.mult))
                chain(eng.tensor_scalar(posm[:, :, 0:NE], w16, 1.0, None, ALU.subtract))
                eng.tensor_copy(cnt[:, 0:NE], bank[6][0:1, 96:112])
                eng.tensor_reduce(cnt[:, NE:NE + NPAIR], bank[6][0:1, 96:112].rearrange("p (a b) -> p a b", b=2),
                                  axis=AX_X, op=ALU.max).then_inc(routed, 1)
                eng.wait_ge(routed, l + 1)

            def one_hot(dst, e, q):
                shape = [P, NS, 2, CAP]
                return eng.tensor_tensor(dst.rearrange("p s (e c) -> p s e c", e=2),
                                         posm[:, :, bass.ds(e, 2)].unsqueeze(3).broadcast_to(shape),
                                         col(C_IOTA + q * CAP, CAP).unsqueeze(1).unsqueeze(1).broadcast_to(shape),
                                         ALU.is_equal)

            def pair(l, p, it=None):
                ln = NPAIR * l
                t = 0 if it is None else 3 * it
                e = 2 * p if it is None else 6 * it + 2 * p

                def tile(j, q):
                    base = 36 * (ln + p) + 18 * j + 6 * q + (0 if it is None else 108 * it)
                    shape = [P, NS, 2, CAP]
                    slots_q = col(C_IOTA + (q + 1) * CAP, CAP)
                    for dst in (o_S, o_Sg):
                        eng.tensor_tensor(dst.rearrange("p s (e c) -> p s e c", e=2),
                                          posm[:, :, bass.ds(e + j, 1)].unsqueeze(3).broadcast_to(shape),
                                          slots_q.unsqueeze(1).unsqueeze(1).broadcast_to(shape),
                                          ALU.is_equal)
                    eng.drain()
                    v = o_Sg.rearrange("p s (e c) -> p s e c", e=2)
                    eng.tensor_tensor(v, v, gt[:, :, bass.ds(e + j, 1)].unsqueeze(3).broadcast_to(shape),
                                      ALU.mult).then_inc(ovf_dve, 1)
                    eng.wait_ge(ovf_pe, base + 1)
                    eng.tensor_copy(xs[:, 0:512], bank[6][:, :]).then_inc(ovf_dve, 1)
                    eng.wait_ge(ovf_pe, base + 2)
                    eng.tensor_copy(hTf[:, 0:512], bank[4][:, :]).then_inc(ovf_dve, 1)
                    eng.wait_ge(ovf_act, 6 * (ln + p) + 3 * j + q + 1 + (0 if it is None else 18 * it))
                    eng.tensor_tensor(act[0:CAP, :], act[0:CAP, :], o_up, ALU.mult).then_inc(ovf_dve, 1)
                    eng.wait_ge(ovf_pe, base + 4)
                    eng.tensor_copy(work[:, 2560:3072], bank[4][:, :])
                    eng.tensor_copy(work[:, 3072:3328], bank[5][:, 0:256]).then_inc(ovf_dve, 1)
                    eng.wait_ge(ovf_pe, base + 5)
                    eng.tensor_copy(ysb[:, 0, :], bank[6][:, :]).then_inc(ovf_dve, 1)

                overflow(eng, ovf_dve, 6, l, p, it, tile)

                eng.wait_ge(gat_done, 2 * t + 2 * (9 * l + p + 1))
                one_hot(S, e + 2, 0).then_inc(S_ready, 1)
                one_hot(Sg, e, 0).then_inc(Sg_half, 1)
                eng.wait_ge(Sg_half, t + (ln + p + 1))
                v = Sg.rearrange("p s (e c) -> p s e c", e=2)
                eng.tensor_tensor(v, v, gt[:, :, bass.ds(e, 2)].unsqueeze(3).broadcast_to([P, NS, 2, CAP]),
                                  ALU.mult).then_inc(Sg_ready, 1)
                eng.wait_ge(silu_done, t + (ln + p + 1))
                eng.wait_ge(up_done, t + (ln + p + 1))
                eng.tensor_tensor(act, act, bank[5][:, :], ALU.mult).then_inc(act_ready, 1)
                eng.wait_ge(actT_psum, 2 * t + (2 * (ln + p) + 1))
                eng.tensor_copy(work[:, 2560:3072], bank[4][:, :]).then_inc(actT_ready, 1)
                eng.wait_ge(actT_psum, 2 * t + (2 * (ln + p) + 2))
                eng.tensor_copy(work[:, 3072:3328], bank[5][:, 0:256]).then_inc(ST_ready, 1)
                eng.wait_ge(down_done, t + (ln + p + 1))
                eng.tensor_copy(ysb[:, 1, :], bank[7][:, :]).then_inc(y_dve, 1)
                eng.wait_ge(xgT_psum, t + (9 * l + p + 2))
                eng.tensor_copy(work[:, 1536:2048], bank[5][:, :]).then_inc(xg_dve, 1)

            def moe(l):
                route(l)
                one_hot(S, 0, 0).then_inc(S_ready, 1)
                eng.wait_ge(xgT_psum, 9 * l + 1)
                eng.tensor_copy(work[:, 1536:2048], bank[5][:, :]).then_inc(xg_dve, 1)
                pair(l, 0)
                pair(l, 1)
                with eng.Fori(0, 2) as it:
                    for p in range(2, 5):
                        pair(l, p, it)

            eng.memset(zero_b[:, :], 0.0)
            eng.memset(rwp[:, :, :], 0.0)
            eng.memset(posm[:, :, :], -1.0)
            eng.memset(gt[:, :, :], 0.0)
            eng.memset(condT[:, :, :], 0.0).then_inc(zeroed, 1)
            eng.wait_ge(tab_in, 16)
            eng.tensor_copy(sel_b[:, :], col(C_SEL, NS * P)).then_inc(sel_ready, 1)
            eng.wait_ge(cond_ready, NPART)
            norm(0, 0)
            norm(0, 1)
            eng.wait_ge(attn_in, 16 * 13)
            eng.tensor_copy(rwp[:, :, 0:NE], rw[:, :, :]).then_inc(rw_ready, 1)
            chain(eng.tensor_tensor(lams[:, 0:128], lams[:, 0:128], lams[:, 128:256], ALU.mult))
            eng.tensor_reduce(lamv[:, 0:2], lams[:, 0:128].rearrange("p (a n) -> p a n", a=2), axis=AX_X,
                              op=ALU.add).then_inc(lam_dots, 1)
            eng.wait_ge(pre_psum, 1)
            eng.tensor_copy(kTs[:, :, 0:P], bank[2][:, :].rearrange("p (h t) -> p h t", h=H)).then_inc(pre_evac, 1)
            eng.wait_ge(pre_psum, 2)
            eng.tensor_copy(work[:, 512:1024], bank[3][:, :]).then_inc(pre_evac, 1)
            for i in range(4):
                t, s = i // 2, i % 2
                eng.wait_ge(win_evac, i + 1)
                v = qk[:, s, t, :]
                v8 = v.rearrange("p (m d) -> p m d", m=8)
                t8 = tmp.rearrange("p (m d) -> p m d", m=8)
                chain(eng.tensor_tensor(tmp, v, v, ALU.mult))
                chain(eng.tensor_reduce(qss, t8, axis=AX_X, op=ALU.add))
                rstd(qss, DH)
                chain(eng.tensor_tensor(v8, v8, qss.unsqueeze(2).broadcast_to([P, 8, DH]), ALU.mult))
                last = eng.tensor_tensor(v8, v8, (qg, kg)[t].unsqueeze(1).broadcast_to([P, 8, DH]), ALU.mult)
                if s == 1:
                    chain(last)
                    r8 = prob[1][:, 0, 0:2, :].rearrange("p a b -> p (a b)").rearrange("p (m d) -> p m d", m=8)
                    eng.tensor_tensor(t8, v8, col(C_COS, 64).unsqueeze(1).broadcast_to([P, 8, 64]), ALU.mult)
                    for half in range(2):
                        for pt in range(2):
                            o, f = 32 * half + 16 * pt, 32 * half + 16 * (1 - pt)
                            last = eng.tensor_tensor(r8[:, :, o:o + 16], v8[:, :, f:f + 16],
                                                     col(C_SIN + o, 16).unsqueeze(1).broadcast_to([P, 8, 16]), ALU.mult)
                    chain(last)
                    last = eng.tensor_tensor(v8, t8, r8, ALU.add)
                last.then_inc(qk_ready, 1)
                eng.wait_ge(qk_ready, i + 1)
            for g in range(4):
                eng.wait_ge(sg_psum, g // 2 + 1)
                mixed = bank[g // 2][:, 256 * (g % 2):256 * (g % 2) + 256].rearrange("p (s n) -> p s n", s=NS)
                eng.scalar_tensor_tensor(h[:, :, 512 + g * P:512 + (g + 1) * P], mixed, sgbT[:, g:g + 1],
                                         gu[:, :, g * P:(g + 1) * P], ALU.add, ALU.mult).then_inc(sg_used, 1)
            for i, dst in enumerate((qT[:, 0, :, :], kTp)):
                eng.wait_ge(qkT_psum, i + 1)
                eng.tensor_copy(dst, bank[2 + i][:, :].rearrange("p (h t) -> p h t", h=H)).then_inc(qkT_dve, 1)
            for g, (s, b0, heads) in enumerate(((0, 0, 4), (1, 2, 2), (1, 4, 2))):
                eng.wait_ge(score_psum, g + 1)
                h0 = 2 if g == 2 else 0
                for cm in range(2):
                    chain(eng.tensor_reduce(mx[:, s, cm, h0:h0 + heads],
                                            bank[b0 + cm][:, :].rearrange("p (h t) -> p h t", h=heads),
                                            axis=AX_X, op=ALU.max))
                m = mx[:, s, :, h0:h0 + heads]
                eng.tensor_scalar(m, m, -(DH ** -0.5), None, ALU.mult).then_inc(mx_ready, 1)
            eng.wait_ge(lam_exp, 1)
            chain(eng.tensor_tensor(lamv[:, 0:1], lamv[:, 2:3], lamv[:, 3:4], ALU.subtract))
            chain(eng.tensor_scalar(lamv[:, 0:1], lamv[:, 0:1], LAM0, None, ALU.add))
            for s in range(NS):
                eng.wait_ge(exp_ready, 1 + 2 * s)
                es = esum[:, s, :, :]
                chain(eng.reciprocal(es, es))
                chain(eng.tensor_scalar(esum[:, s, 1, :], esum[:, s, 1, :], lamv[:, 0:1], None, ALU.mult))
                for hh in range(H):
                    p0, p1 = prob[s][:, 0, hh, :], prob[s][:, 1, hh, :]
                    chain(eng.tensor_scalar(p1, p1, esum[:, s, 1, hh:hh + 1], None, ALU.mult))
                    eng.scalar_tensor_tensor(p0, p0, esum[:, s, 0, hh:hh + 1], p1, ALU.mult,
                                             ALU.subtract).then_inc(a_map, 1)
            eng.wait_ge(oss_ready, NS)
            rstd(oss, P)
            for s in range(NS):
                h4 = h[:, s, 0:512].rearrange("p (h n) -> p h n", h=H)
                chain(eng.tensor_tensor(h4, bank[3 + s][:, :].rearrange("p (h n) -> p h n", h=H),
                                        oss[:, H * s:H * (s + 1)].unsqueeze(2).broadcast_to([P, H, P]), ALU.mult))
                eng.scalar_tensor_tensor(h4, h4, 1.0 - LAM0, subg.unsqueeze(1).broadcast_to([P, H, P]),
                                         ALU.mult, ALU.mult).then_inc(att_ready, 1)
            split(1)
            residual(0, 0)
            eng.wait_ge(tr_psum, 8)
            norm(1, 0)
            residual(0, 1)
            norm(1, 1)
            moe(0)
            residual(1, 0)
            residual(1, 1)
            norm(2, 0)
            norm(2, 1)
            split(4)
            residual(2, 0)
            residual(2, 1)
            norm(3, 0)
            norm(3, 1)
            moe(1)
            residual(3, 0)
            residual(3, 1)


_INS = ['x_prompt', 'x_sample', 'cache_k', 'cache_v', 'c', 'c_ctx', 'norm1_g', 'norm2_g', 'w_ada', 'b_ada',
        'w_in', 'w_out', 'q_norm_g', 'k_norm_g', 'lam_q1', 'lam_k1', 'lam_q2', 'lam_k2', 'subln_g',
        'sg_w', 'sg_b', 'pool_w', 'pool_scale', 'router_w', 'router_b', 'w_gate', 'w_up', 'w_down']
_OUTS = [(1, P, D), (1, P, D), (1, 1, P, H, 2, DH), (1, 1, P, H, 2 * DH)]


def kernel(**inputs):
    import numpy as _np
    import concourse.bacc as _bacc
    from concourse import mybir as _mybir
    from concourse.bass_utils import run_bass_kernel_spmd as _run

    nc = _bacc.Bacc("TRN2", target_bir_lowering=False, num_devices=1)
    arrays, args = {}, []
    for name in _INS:
        a = _np.asarray(inputs[name])
        a = _np.ascontiguousarray(a.transpose(0, 2, 1) if name == "sg_b" else a)
        arrays[f"in_{name}_dram"] = a
        args.append(nc.dram_tensor(f"in_{name}_dram", a.shape, _mybir.dt.from_np(a.dtype), kind="ExternalInput").ap())
    t = constant_table()
    arrays["in_table_dram"] = t
    args.append(nc.dram_tensor("in_table_dram", t.shape, _mybir.dt.float32, kind="ExternalInput").ap())
    for i, shape in enumerate(_OUTS):
        args.append(nc.dram_tensor(f"out_{i}_dram", shape, _mybir.dt.float32, kind="ExternalOutput").ap())
    trunk_kernel(nc, *args)
    r = _run(nc, [arrays], core_ids=[0])
    return tuple(r.results[0][f"out_{i}_dram"] for i in range(len(_OUTS)))
```
